# Optimizing a Trainium2 kernel written in Bass

```python
import jax, jax.numpy as jnp
from jax import lax
import numpy as np

D_MODEL = 1024
BATCH = 1
SEQ = 512
DEPTH = 2
DEC_BATCH = 8
DEC_SEQ = 4
PAST_LEN = 1024
PAGE_SIZE = 128

HEAD_DIM = 64
N_HEADS_A = 8
N_KV_A = 2
KV_REP = N_HEADS_A // N_KV_A
WINDOW = 128
ROT_DIM = HEAD_DIM // 4
ROPE_THETA = 500000.0
ATTN_SCALE = HEAD_DIM ** -0.5
NEG_INF = -1e30
N_HEADS_B = 4
DK_B = 128
DV_B = 128
HGRN_CHUNK = 64
N_B_LAYERS = (DEPTH + 1) // 2
CONV_W = 31
N_KEYS = 128
N_EXPERTS = N_KEYS * N_KEYS
PEER_HEADS = 8
PEER_TOPK = 16
PEER_DKH = 128
PEER_BLOCK = 256
NORM_EPS = 1e-6

QA = N_HEADS_A * HEAD_DIM
KVA = N_KV_A * HEAD_DIM
QB = N_HEADS_B * DK_B
VB = N_HEADS_B * DV_B
IN0_SPLITS = (QA, QA + KVA, QA + 2 * KVA, QA + 2 * KVA + QB, QA + 2 * KVA + 2 * QB, QA + 2 * KVA + 2 * QB + VB)
IN0_WIDTH = QA + 2 * KVA + 2 * QB + 2 * VB
MIX0_WIDTH = QA + VB

kernel_name = 'hybrid_swa_hgrn2_conformer_peer_step'

def rms_norm(x, g):
    xf = x.astype(jnp.float32)
    y = xf * lax.rsqrt(jnp.mean(xf * xf, axis=-1, keepdims=True) + NORM_EPS)
    return (y * g.astype(jnp.float32)).astype(x.dtype)

def rope_partial(x, pos):
    inv = ROPE_THETA ** (-jnp.arange(0, ROT_DIM, 2, dtype=jnp.float32) / ROT_DIM)
    ang = pos[:, None] * inv[None, :]
    c = jnp.cos(ang)[:, None, :]
    s = jnp.sin(ang)[:, None, :]
    xf = x.astype(jnp.float32)
    half = ROT_DIM // 2
    x1 = xf[..., :half]
    x2 = xf[..., half:ROT_DIM]
    out = jnp.concatenate([x1 * c - x2 * s, x2 * c + x1 * s, xf[..., ROT_DIM:]], axis=-1)
    return out.astype(x.dtype)

def sink_softmax(s, mask, sinks):
    s = jnp.where(mask, s, NEG_INF)
    sk = jnp.broadcast_to(sinks.astype(jnp.float32).reshape(N_KV_A, KV_REP, 1, 1), s.shape[:-1] + (1,))
    p = jax.nn.softmax(jnp.concatenate([s, sk], axis=-1), axis=-1)
    return p[..., :-1]

def swa_prompt(q, k, v, sinks):
    B, T = q.shape[0], q.shape[1]
    nb = T // WINDOW
    qb = q.reshape(B, nb, WINDOW, N_KV_A, KV_REP, HEAD_DIM)

    def with_prev(xb):
        prev = jnp.concatenate([jnp.zeros_like(xb[:, :1]), xb[:, :-1]], axis=1)
        return jnp.concatenate([prev, xb], axis=2)

    kk = with_prev(k.reshape(B, nb, WINDOW, N_KV_A, HEAD_DIM))
    vv = with_prev(v.reshape(B, nb, WINDOW, N_KV_A, HEAD_DIM))
    s = jnp.einsum('bnqgrd,bnkgd->bngrqk', qb, kk, preferred_element_type=jnp.float32) * ATTN_SCALE
    qi = jnp.arange(WINDOW)[:, None]
    ki = jnp.arange(2 * WINDOW)[None, :]
    dist = qi + WINDOW - ki
    blk = jnp.arange(nb)[:, None, None]
    mask = (dist >= 0) & (dist < WINDOW) & ((blk > 0) | (ki >= WINDOW))
    p = sink_softmax(s, mask[None, :, None, None], sinks)
    o = jnp.einsum('bngrqk,bnkgd->bnqgrd', p.astype(v.dtype), vv)
    return o.reshape(B, T, QA)

def swa_decode(q, k, v, k_past, v_past, sinks):
    B, T = q.shape[0], q.shape[1]
    wb = k_past.shape[1]
    kk = jnp.concatenate([k_past.astype(k.dtype), k], axis=1)
    vv = jnp.concatenate([v_past.astype(v.dtype), v], axis=1)
    qg = q.reshape(B, T, N_KV_A, KV_REP, HEAD_DIM)
    s = jnp.einsum('btgrd,bkgd->bgrtk', qg, kk, preferred_element_type=jnp.float32) * ATTN_SCALE
    dist = (wb + jnp.arange(T))[:, None] - jnp.arange(wb + T)[None, :]
    mask = (dist >= 0) & (dist < WINDOW)
    p = sink_softmax(s, mask, sinks)
    o = jnp.einsum('bgrtk,bkgd->btgrd', p.astype(v.dtype), vv).reshape(B, T, QA)
    return o, kk[:, -wb:], vv[:, -wb:]

def hgrn_scan(q, k, i, logf, s0):
    B, H, T = q.shape[0], q.shape[1], q.shape[2]
    C = min(HGRN_CHUNK, T)
    n = -(-T // C)
    pad = n * C - T

    def prep(x):
        x = jnp.pad(x, ((0, 0), (0, 0), (0, pad), (0, 0)))
        return jnp.moveaxis(x.reshape(B, H, n, C, x.shape[-1]), 2, 0)

    tril = jnp.tril(jnp.ones((C, C), dtype=bool))[:, :, None]

    def step(S, xs):
        qc, kc, ic, lc = xs
        b = jnp.cumsum(lc, axis=2)
        o = jnp.einsum('bhtk,bhkv->bhtv', qc * jnp.exp(b), S)
        diff = b[:, :, :, None, :] - b[:, :, None, :, :]
        decay = jnp.where(tril, jnp.exp(jnp.where(tril, diff, 0.0)), 0.0)
        a = jnp.einsum('bhtk,bhtsk,bhsk->bhts', qc, decay, kc)
        o = o + jnp.einsum('bhts,bhsv->bhtv', a, ic)
        bl = b[:, :, -1:, :]
        S = jnp.exp(bl[:, :, 0, :, None]) * S + jnp.einsum('bhsk,bhsv->bhkv', kc * jnp.exp(bl - b), ic)
        return S, o

    S, o = lax.scan(step, s0, (prep(q), prep(k), prep(i), prep(logf)))
    o = jnp.moveaxis(o, 0, 2).reshape(B, H, n * C, i.shape[-1])[:, :, :T]
    return o, S

def even_mixer(h, pos, k_past, v_past, s_past, b_idx, w_in0, attn_q_norm_g, attn_k_norm_g, attn_sinks,
               hgrn_lb, hgrn_o_norm_g, w_out0):
    B, T = h.shape[0], h.shape[1]
    z = h @ w_in0
    qa, ka, va, qb, fb, ib, gb = jnp.split(z, IN0_SPLITS, axis=-1)
    q = rope_partial(rms_norm(qa.reshape(B, T, N_HEADS_A, HEAD_DIM), attn_q_norm_g), pos)
    k = rope_partial(rms_norm(ka.reshape(B, T, N_KV_A, HEAD_DIM), attn_k_norm_g), pos)
    v = va.reshape(B, T, N_KV_A, HEAD_DIM)
    if k_past is None:
        attn = swa_prompt(q, k, v, attn_sinks)
        k_win, v_win = k[:, -WINDOW:], v[:, -WINDOW:]
    else:
        attn, k_win, v_win = swa_decode(q, k, v, k_past, v_past, attn_sinks)
    lb = jnp.cumsum(jax.nn.softmax(hgrn_lb.astype(jnp.float32), axis=0), axis=0)[b_idx].reshape(N_HEADS_B, DK_B)
    fr = fb.astype(jnp.float32).reshape(B, T, N_HEADS_B, DK_B)
    logf = jnp.log(lb + (1.0 - lb) * jax.nn.sigmoid(fr))
    kb = (1.0 - lb) * jax.nn.sigmoid(-fr)
    qh = jax.nn.silu(qb.astype(jnp.float32)).reshape(B, T, N_HEADS_B, DK_B)
    ih = ib.astype(jnp.float32).reshape(B, T, N_HEADS_B, DV_B)
    s0 = jnp.zeros((B, N_HEADS_B, DK_B, DV_B), jnp.float32) if s_past is None else s_past.astype(jnp.float32)
    tr = lambda x: x.transpose(0, 2, 1, 3)
    o, s_new = hgrn_scan(tr(qh), tr(kb), tr(ih), tr(logf), s0)
    o = rms_norm(tr(o), hgrn_o_norm_g) * jax.nn.silu(gb.astype(jnp.float32).reshape(B, T, N_HEADS_B, DV_B))
    hg = o.reshape(B, T, VB).astype(h.dtype)
    out = jnp.concatenate([attn, hg], axis=-1) @ w_out0
    return out, k_win, v_win, s_new.astype(h.dtype)

def conv_mixer(h, buf, conv_w_pw1, conv_b_pw1, conv_w_dw, conv_b_dw, conv_ln_g, conv_ln_b, conv_w_pw2):
    B = h.shape[0]
    a = h @ conv_w_pw1 + conv_b_pw1
    u = a[..., :D_MODEL] * jax.nn.sigmoid(a[..., D_MODEL:])
    if buf is None:
        buf = jnp.zeros((B, CONV_W - 1, D_MODEL), u.dtype)
    up = jnp.concatenate([buf.astype(u.dtype), u], axis=1)
    c = lax.conv_general_dilated(up, conv_w_dw[:, None, :].astype(up.dtype), (1,), 'VALID',
                                 dimension_numbers=('NWC', 'WIO', 'NWC'),
                                 feature_group_count=D_MODEL) + conv_b_dw
    cf = c.astype(jnp.float32)
    mu = jnp.mean(cf, axis=-1, keepdims=True)
    var = jnp.mean(jnp.square(cf - mu), axis=-1, keepdims=True)
    ln = (cf - mu) * lax.rsqrt(var + NORM_EPS) * conv_ln_g.astype(jnp.float32) + conv_ln_b.astype(jnp.float32)
    y = jax.nn.silu(ln).astype(h.dtype) @ conv_w_pw2
    return y, up[:, -(CONV_W - 1):]

def peer(h, w_q, sub_keys, u_tab, v_tab):
    B, T, D = h.shape
    n = B * T
    blk = min(PEER_BLOCK, n)
    nb = -(-n // blk)
    xs = jnp.pad(h.reshape(n, D), ((0, nb * blk - n), (0, 0))).reshape(nb, blk, D)

    def block(xb):
        q = (xb @ w_q).reshape(blk, PEER_HEADS, 2, PEER_DKH)
        sc = jnp.einsum('nhpd,hpkd->nhpk', q, sub_keys, preferred_element_type=jnp.float32)
        sv, si = lax.top_k(sc, PEER_TOPK)
        cand = (sv[:, :, 0, :, None] + sv[:, :, 1, None, :]).reshape(blk, PEER_HEADS, PEER_TOPK * PEER_TOPK)
        cidx = (si[:, :, 0, :, None] * N_KEYS + si[:, :, 1, None, :]).reshape(blk, PEER_HEADS, PEER_TOPK * PEER_TOPK)
        fv, fi = lax.top_k(cand, PEER_TOPK)
        eidx = jnp.take_along_axis(cidx, fi, axis=-1)
        gate = jax.nn.softmax(fv, axis=-1)
        uu = jnp.take(u_tab, eidx, axis=0)
        act = jax.nn.gelu(jnp.einsum('nd,nhed->nhe', xb, uu).astype(jnp.float32), approximate=False)
        vv = jnp.take(v_tab, eidx, axis=0)
        return jnp.einsum('nhe,nhed->nd', (gate * act).astype(xb.dtype), vv)

    y = lax.map(block, xs).reshape(nb * blk, D)[:n]
    return y.reshape(B, T, D)

def trunk(x, pos, k_past, v_past, s_past, conv_past, norm_mix_g, norm_ffn_g, w_in0, attn_q_norm_g,
          attn_k_norm_g, attn_sinks, hgrn_lb, hgrn_o_norm_g, w_out0, conv_w_pw1, conv_b_pw1, conv_w_dw,
          conv_b_dw, conv_ln_g, conv_ln_b, conv_w_pw2, peer_w_q, peer_keys, peer_u, peer_v):
    for l in range(DEPTH):
        h = rms_norm(x, norm_mix_g[l])
        if l % 2 == 0:
            m, k_win, v_win, s_new = even_mixer(h, pos, k_past, v_past, s_past, l // 2, w_in0, attn_q_norm_g,
                                                attn_k_norm_g, attn_sinks, hgrn_lb, hgrn_o_norm_g, w_out0)
        else:
            m, conv_new = conv_mixer(h, conv_past, conv_w_pw1, conv_b_pw1, conv_w_dw, conv_b_dw,
                                     conv_ln_g, conv_ln_b, conv_w_pw2)
        x = x + m.astype(x.dtype)
        x = x + peer(rms_norm(x, norm_ffn_g[l]), peer_w_q[l], peer_keys[l], peer_u[l], peer_v[l]).astype(x.dtype)
    return x, k_win, v_win, s_new, conv_new

def setup_inputs(seed: int = 0) -> dict:
    key = jax.random.key(seed)
    ks = jax.random.split(key, 26)
    f32 = jnp.float32
    nrm = lambda k, shape, scale: jax.random.normal(k, shape, f32) * scale
    return {
        'x_prompt': nrm(ks[0], (BATCH, SEQ, D_MODEL), 1.0),
        'x_sample': nrm(ks[1], (DEC_BATCH, DEC_SEQ, D_MODEL), 1.0),
        'cache_swa_k': nrm(ks[2], (DEC_BATCH, WINDOW, N_KV_A, HEAD_DIM), 1.0),
        'cache_swa_v': nrm(ks[3], (DEC_BATCH, WINDOW, N_KV_A, HEAD_DIM), 1.0),
        'state_hgrn': nrm(ks[4], (DEC_BATCH, N_HEADS_B, DK_B, DV_B), 0.5),
        'state_conv': nrm(ks[5], (DEC_BATCH, CONV_W - 1, D_MODEL), 0.5),
        'norm_mix_g': 1.0 + nrm(ks[6], (DEPTH, D_MODEL), 0.05),
        'norm_ffn_g': 1.0 + nrm(ks[7], (DEPTH, D_MODEL), 0.05),
        'w_in0': nrm(ks[8], (D_MODEL, IN0_WIDTH), D_MODEL ** -0.5),
        'attn_q_norm_g': 1.0 + nrm(ks[9], (HEAD_DIM,), 0.05),
        'attn_k_norm_g': 1.0 + nrm(ks[10], (HEAD_DIM,), 0.05),
        'attn_sinks': nrm(ks[11], (N_HEADS_A,), 0.5),
        'hgrn_lb': nrm(ks[12], (N_B_LAYERS + 1, QB), 0.5),
        'hgrn_o_norm_g': 1.0 + nrm(ks[13], (DV_B,), 0.05),
        'w_out0': nrm(ks[14], (MIX0_WIDTH, D_MODEL), MIX0_WIDTH ** -0.5),
        'conv_w_pw1': nrm(ks[15], (D_MODEL, 2 * D_MODEL), D_MODEL ** -0.5),
        'conv_b_pw1': nrm(ks[16], (2 * D_MODEL,), 0.02),
        'conv_w_dw': nrm(ks[17], (CONV_W, D_MODEL), CONV_W ** -0.5),
        'conv_b_dw': nrm(ks[18], (D_MODEL,), 0.02),
        'conv_ln_g': 1.0 + nrm(ks[19], (D_MODEL,), 0.05),
        'conv_ln_b': nrm(ks[20], (D_MODEL,), 0.02),
        'conv_w_pw2': nrm(ks[21], (D_MODEL, D_MODEL), D_MODEL ** -0.5),
        'peer_w_q': nrm(ks[22], (DEPTH, D_MODEL, PEER_HEADS * 2 * PEER_DKH), D_MODEL ** -0.5),
        'peer_keys': nrm(ks[23], (DEPTH, PEER_HEADS, 2, N_KEYS, PEER_DKH), PEER_DKH ** -0.5),
        'peer_u': nrm(ks[24], (DEPTH, N_EXPERTS, D_MODEL), D_MODEL ** -0.5),
        'peer_v': nrm(ks[25], (DEPTH, N_EXPERTS, D_MODEL), PEER_HEADS ** -0.5),
    }

def reference(x_prompt, x_sample, cache_swa_k, cache_swa_v, state_hgrn, state_conv, norm_mix_g, norm_ffn_g,
              w_in0, attn_q_norm_g, attn_k_norm_g, attn_sinks, hgrn_lb, hgrn_o_norm_g, w_out0, conv_w_pw1,
              conv_b_pw1, conv_w_dw, conv_b_dw, conv_ln_g, conv_ln_b, conv_w_pw2, peer_w_q, peer_keys,
              peer_u, peer_v):
    pos_p = jnp.arange(x_prompt.shape[1], dtype=jnp.float32)
    pos_s = PAST_LEN + jnp.arange(x_sample.shape[1], dtype=jnp.float32)
    y_prompt, k_win_prompt, v_win_prompt, s_hgrn_prompt, conv_buf_prompt = trunk(
        x_prompt, pos_p, None, None, None, None, norm_mix_g, norm_ffn_g, w_in0, attn_q_norm_g,
        attn_k_norm_g, attn_sinks, hgrn_lb, hgrn_o_norm_g, w_out0, conv_w_pw1, conv_b_pw1, conv_w_dw,
        conv_b_dw, conv_ln_g, conv_ln_b, conv_w_pw2, peer_w_q, peer_keys, peer_u, peer_v)
    y_sample, k_win_sample, v_win_sample, s_hgrn_sample, conv_buf_sample = trunk(
        x_sample, pos_s, cache_swa_k, cache_swa_v, state_hgrn, state_conv, norm_mix_g, norm_ffn_g, w_in0,
        attn_q_norm_g, attn_k_norm_g, attn_sinks, hgrn_lb, hgrn_o_norm_g, w_out0, conv_w_pw1, conv_b_pw1,
        conv_w_dw, conv_b_dw, conv_ln_g, conv_ln_b, conv_w_pw2, peer_w_q, peer_keys, peer_u, peer_v)
    return (y_prompt, y_sample, k_win_prompt, v_win_prompt, s_hgrn_prompt, conv_buf_prompt,
            k_win_sample, v_win_sample, s_hgrn_sample, conv_buf_sample)


_drawn_inputs = setup_inputs


def setup_inputs(seed=0):
    import zlib

    import numpy as np

    out = dict(_drawn_inputs(seed))
    spreads = {}
    factors = {'attn_sinks': 4.58, 'conv_b_pw1': 2.703, 'conv_ln_b': 3.026}
    for name, (base, spread) in spreads.items():
        noise = np.random.default_rng([zlib.crc32(name.encode()), seed]).standard_normal(out[name].shape)
        drawn = base * np.exp(spread * noise) if base else spread * noise
        out[name] = __import__('jax').numpy.asarray(drawn.astype(out[name].dtype))
    for name, factor in factors.items():
        out[name] = (out[name] * factor).astype(out[name].dtype)
    return out
```

```python
from contextlib import ExitStack

import concourse.bass as bass
from concourse import mybir

F32 = mybir.dt.float32
F32R = mybir.dt.float32r
U32 = mybir.dt.uint32
ALU = mybir.AluOpType
ACT = mybir.ActivationFunctionType
X = mybir.AxisListType.X

P = 128
D = 1024
KC = D // P
NP, NS, SB, ST = 512, 32, 8, 4
NT = NP + NS
HALF = NT // 2
NTILE = 5
ROWS = [128, 128, 128, 128, 32]
EPS = 1e-6
HD, WIN = 64, 128
HPEER, TOPK, NKEY = 8, 16, 128
NBLK = NP // P
CW = 31
SCALE = HD ** -0.5

T_IN, N_IN = 0, 22
T_OUT, N_OUT = 22, 8
T_WQ = [30, 342 - 16]
N_WQ = 16
T_EXP = [46, 342]
N_EXP = 256
T_PW1, T_PW2 = 302, 318
N_TILES = 598
GRP = 4
NG = NKEY // GRP
LOOK = 4
SLOTS = 8

CAND_W = [TOPK // (a + 1) for a in range(TOPK)]
CAND_AT = [sum(CAND_W[:a]) for a in range(TOPK)]
NCAND = sum(CAND_W)

CHUNKS = [(16 * c, 16) for c in range(NP // 16)] + [(NP + ST * b, ST) for b in range(SB)]
NPC = NP // 16
NCH = len(CHUNKS)

PC = {}
_at = 0
for _n, _w in (("g_mix0", 8), ("g_ffn0", 8), ("g_mix1", 8), ("g_ffn1", 8), ("gq", 1), ("gk", 1), ("sink", 8),
               ("sinkd", 1), ("lb0", 4), ("lb1", 4), ("og", 1), ("b1", 16), ("wdw", 8 * CW), ("bdw", 8),
               ("lng", 8), ("lnb", 8)):
    PC[_n] = (_at, _w)
    _at += _w
NPAR = _at
CC = {"ident": (0, 128), "ones": (128, 128), "iota": (256, 128), "start": (384, 15), "dstart": (399, 15)}
NCON = 414
MC = {"blk": (0, 128), "rot": (128, 128), "band": (256, 256), "band0": (512, 256), "dec": (768, 132),
      "tri": (900, 64), "cos": (964, NT), "sin": (964 + NT, NT)}
NMC = 964 + 2 * NT


def build(nc, xT, stream, params, consts, mconsts, reset, keysT, kcacheT, vcache, kvcache_n, state_h, convT,
          yT, kwin_p, vwin_p, hs_p, cb_p, kwin_s, vwin_s, hs_s, cb_s):
    ctx = ExitStack()
    with ctx:
        def sb(name, shape, dt=F32, where=ctx):
            return where.enter_context(nc.sbuf_tensor(name, shape, dt))

        def sem(name):
            return ctx.enter_context(nc.semaphore(name))

        xt = sb("xt", [P, KC, NT])
        hh = sb("hh", [P, KC, NT], F32R)
        hl = sb("hl", [P, KC, NT], F32R)
        raw = [sb(f"raw{i}", [P, D]) for i in range(2)]
        par = sb("par", [P, NPAR])
        con = sb("con", [P, NCON])
        small = sb("small", [P, 64])
        root = sb("root", [P, NT])
        eps = small[:, 0:1]

        def pc(n, i=0, w=1):
            return par[:, PC[n][0] + i:PC[n][0] + i + w]

        def cc(n):
            return con[:, CC[n][0]:CC[n][0] + CC[n][1]]
        ident, ones, iota = cc("ident"), cc("ones"), cc("iota")

        with ExitStack() as z:
            ring_hi = sb("ring_hi", [P, SLOTS, D], F32R, z)
            ring_lo = sb("ring_lo", [P, SLOTS, D], F32R, z)
        with ExitStack() as z:
            hK = sb("hK", [P, 4, NT], F32, z)
            hQ1 = sb("hQ1", [P, 4, NT], F32, z)
            hK1 = sb("hK1", [P, 4, NT], F32, z)
            hT1 = sb("hT1", [P, 4, NT], F32, z)
            hT2 = sb("hT2", [P, 4, NT], F32, z)
            hD = sb("hD", [P, 4, NCH], F32, z)
            am = sb("am", [16, 2, 4, 16], F32, z)
            with ExitStack() as zz:
                hO = sb("hO", [P, 4, NT], F32, zz)
                kiT = sb("kiT", [16, 2, 2, 4, P], F32, zz)
            with ExitStack() as zz:
                kcat = sb("kcat", [P, SB, WIN + ST], F32, zz)
                vcat = sb("vcat", [P, SB, P], F32, zz)
                vnew = sb("vnew", [ST, SB, P], F32, zz)
                qbd = sb("qbd", [P, SB, 2, 4, ST], F32, zz)
                pd = sb("pd", [P, 2, WIN + ST], F32, zz)
                pdT = sb("pdT", [P, 2, P], F32, zz)
                pdN = sb("pdN", [ST, 2, P], F32, zz)
        with ExitStack() as z:
            stage = sb("stage", [P, NKEY, P], F32, z)
        zone = sb("zone", [P, SLOTS * 2 * D])

        with ExitStack() as z:
            gates = sb("gates", [P, 16, NT], F32, z)
            hf_mix = gates[:, 0:8, :]
            zq = sb("zq", [P, 5, NT], F32, z)
            krp = sb("krp", [P, P + NT], F32, z)
            krz = sb("krz", [P, 2, P + NT], F32, z)
            vT = sb("vT", [P, NT], F32, z)
            vtok = sb("vtok", [P, NBLK + 1, P], F32, z)
            kvo = sb("kvo", [P, 3, P], F32, z)
            mc = sb("mc", [P, NMC], F32, z)
            scr = sb("scr", [P, 4, NT], F32, z)
            scr1 = scr[:, :, :].rearrange("p a n -> p (a n)")
            st8 = sb("st8", [P, 2, 16], F32, z)
        sqz = [scr[:, 0, :], scr[:, 1, :]]
        rt, rt2 = scr[:, 2, :], scr[:, 3, :]
        sm = [scr1[:, 512 * i:512 * i + 512].rearrange("p (g k) -> p g k", g=2) for i in range(2)]
        pT = [scr1[:, 1024 + 512 * i:1536 + 512 * i].rearrange("p (a q) -> p a q", a=4) for i in range(2)]
        S = scr1[:, 0:512].rearrange("p (h v) -> p h v", h=4)
        Ssm = [scr1[:, 512 * (i + 1):512 * (i + 2)].rearrange("p (h v) -> p h v", h=4) for i in range(2)]

        def mcc(n):
            return mc[:, MC[n][0]:MC[n][0] + MC[n][1]]
        resm = mcc("cos")
        with ExitStack() as z:
            with ExitStack() as zz:
                hf_peer = sb("hf_peer", [P, KC, NT], F32, zz)
            with ExitStack() as zz:
                oh2 = sb("oh2", [P, 2, 8, P], F32, zz)
                oh1 = sb("oh1", [P, 2, 8, P], F32, zz)
            sb("ohpad", [P, KC * NT], F32, z)
            keys = sb("keys", [P, 16, P], F32, z)
            qh = sb("qh", [P, 2, NT], F32, z)
            sc2 = sb("sc2", [P, NTILE, P], F32, z)
            sv = sb("sv", [P, NTILE, 16, 16], F32, z)
            si = sb("si", [P, NTILE, 16, 16], U32, z)
            sif = sb("sif", [P, 16, 16], F32, z)
            cand = sb("cand", [P, 8, NCAND], F32, z)
            cand2 = sb("cand2", [P, 8, NCAND], F32, z)
            fv = sb("fv", [P, 8, 16], F32, z)
            fi = sb("fi", [P, 8, 16], U32, z)
            pos = sb("pos", [P, 8, 16], F32, z)
            dsi = sb("dsi", [P, 8, 15], F32, z)
            ge = sb("ge", [P, 4, 16, 16], F32, z)
            tm = sb("tm", [P, 4, 16, 16], F32, z)
            sel = sb("sel", [P, 3, 8, 16], F32, z)
            r16 = sb("r16", [P, 8, 16], F32, z)
            r8 = sb("r8", [P, 2, 8], F32, z)
            slT = sb("slT", [P, 3, NT], F32, z)
        with ExitStack() as z:
            wh = sb("wh", [P, 5, NT], F32R, z)
            wl = sb("wl", [P, 5, NT], F32R, z)
            gt = sb("gt", [P, GRP, NT], F32, z)
            ga = sb("ga", [P, 2, NT], F32, z)
        with ExitStack() as z:
            up = sb("up", [P, KC, CW - 1 + NP], F32, z)
            us = sb("us", [P, KC, SB, CW - 1 + ST], F32, z)
            cv = sb("cv", [P, KC, NT], F32, z)
            hf_conv = sb("hf_conv", [P, KC, NT], F32, z)
            sg = sb("sg", [P, 2, NT], F32, z)
        sb("arena", [P, 19800])

        psum = [ctx.enter_context(nc.psum_tensor(f"bank{i}", [P, 2, 512], F32)) for i in range(4)]
        PA, PB = psum[0:2], psum[2:4]

        def tok2(ap):
            return ap.rearrange("p (a n) -> p a n", a=2)

        def both(pair):
            return pair[:, :, 0:HALF]

        gdram = nc.dram_tensor("gate_matrix", [2, NKEY, P, NT], F32, kind="Internal").ap()

        s_par = sem("params_loaded")
        s_x = sem("x_loaded")
        s_mc = sem("mixer_consts_loaded")
        s_keys = sem("keys_loaded")
        s_dload = sem("decode_cache_loaded")
        s_reset = sem("reset_mask_loaded")
        s_conv = sem("conv_state_loaded")
        s_raw = [sem(f"raw{i}_loaded") for i in range(2)]
        s_hi = sem("hi_ready")
        s_lo = sem("lo_ready")
        s_used = sem("tile_used")
        s_eps = sem("small_consts_ready")
        s_sq = sem("squares_ready")
        s_sum = sem("norm_sum_done")
        s_root = sem("norm_root_ready")
        s_hf = sem("normed_ready")
        s_hh = sem("normed_hi_ready")
        s_hl = sem("normed_lo_ready")
        s_ev = sem("projection_evacuated")
        s_res = sem("residual_added")
        s_v = sem("dve_chain")
        s_a = sem("act_chain")
        s_out = sem("outputs_written")

        V = nc.vector
        A = nc.scalar
        T = nc.tensor

        class Chain:
            def __init__(self, eng, s):
                self.eng, self.s, self.n = eng, s, 0

            def done(self, ins):
                self.n += 1
                ins.then_inc(self.s, 1)

            def sync(self):
                self.eng.wait_ge(self.s, self.n)

            def step(self, ins):
                self.done(ins)
                self.sync()

        block = ctx.enter_context(nc.Block())

        @block.sync
        def _(sp):
            sp.dma_start(xt[:], xT.rearrange("(k p) n -> p k n", p=P)).then_inc(s_x, 16)
            for t in range(2):
                sp.dma_start(raw[t][:], stream[t]).then_inc(s_raw[t], 16)
            with sp.Fori(1, N_TILES // 2) as i:
                for u in range(2):
                    sp.wait_ge(s_lo, 2 * i + u - 1)
                    sp.dma_start(raw[u][:], stream[bass.ds(2 * i + u, 1)].rearrange("a p n -> (a p) n"))\
                      .then_inc(s_raw[u], 16)

        s_qsum = sem("qk_sum_done")
        s_qroot = sem("qk_root_ready")
        s_qn = sem("qk_normed")
        s_qrot = sem("qk_rotated")
        s_qr = sem("qk_roped")
        s_vt = sem("v_transposed")
        s_vev = sem("v_tokens_ready")
        s_pad = sem("pads_zeroed")
        s_s = sem("scores_done")
        s_sm = sem("masked_scores_ready")
        s_nm = sem("neg_max_ready")
        s_pe = sem("exps_ready")
        s_p = sem("probs_ready")
        s_t = sem("probs_transposed")
        s_pt = sem("probs_T_ready")
        s_o = sem("attn_done")
        s_oe = sem("attn_evacuated")
        s_dq = sem("decode_q_ready")
        s_dvt = sem("decode_v_transposed")
        s_dv = sem("decode_v_ready")
        s_ds = sem("decode_scores_done")
        s_dnm = sem("decode_neg_max_ready")
        s_de = sem("decode_exps_ready")
        s_dp = sem("decode_probs_ready")
        s_dt = sem("decode_probs_transposed")
        s_dpt = sem("decode_probs_T_ready")
        s_do = sem("decode_attn_done")
        s_dend = sem("decode_attn_stored")
        s_h = sem("hgrn_operands_ready")
        s_hd = sem("hgrn_dve_stage")
        s_lbx = sem("lower_bound_shifted")
        s_lb = sem("lower_bound_exps_ready")
        s_ha = sem("hgrn_act_stage")
        s_tr = sem("chunk_transposed")
        s_ki = sem("chunk_T_ready")
        s_at = sem("chunk_scores_done")
        s_am = sem("chunk_scores_masked")
        s_oc = sem("chunk_out_done")
        s_oce = sem("chunk_out_evacuated")
        s_kv = sem("chunk_kv_done")
        s_S = sem("state_updated")
        s_sl = [sem(f"sample_state_loaded{i}") for i in range(2)]
        s_so = [sem(f"sample_state_stored{i}") for i in range(2)]
        s_hsq = sem("head_squares_ready")
        s_hs = sem("head_sum_done")
        s_hr = sem("head_root_ready")
        s_mixf = sem("mixer_out_ready")
        s_sc = sem("key_scores_done")
        s_scf = sem("key_scores_read")
        s_gx = sem("gate_shifted")
        s_ge = sem("gate_exp_ready")
        s_sel = sem("selection_ready")
        s_selT = sem("selection_transposed")
        s_slT = sem("selection_T_ready")
        s_oh = sem("onehots_ready")
        s_gm = sem("gate_tokens_done")
        s_gs = sem("gate_tokens_staged")
        s_gw = sem("gate_matrix_written")
        s_gld = [sem(f"gate_tile{i}_loaded") for i in range(GRP)]
        s_ga = sem("gelu_ready")
        s_w = sem("gated_ready")
        s_wh = sem("gated_hi_ready")
        s_wl = sem("gated_lo_ready")
        s_y = sem("expert_out_done")
        s_ya = sem("expert_out_added")
        s_sg = sem("glu_sigmoid_ready")
        s_u = sem("glu_ready")
        s_cv = sem("conv_done")
        s_ms = sem("mean_sum_done")
        s_cen = sem("centered")
        s_csq = sem("centered_squares_ready")
        s_vs = sem("var_sum_done")
        s_cr = sem("ln_root_ready")
        s_ln = sem("ln_ready")
        s_si = sem("ln_silu_ready")

        def wait_x(eng, n):
            if n == 0:
                eng.wait_ge(s_x, 16)
            elif n == 1:
                eng.wait_ge(s_res, 8)
            elif n == 2:
                eng.wait_ge(s_ya, 8 * NG)
            else:
                eng.wait_ge(s_res, 16)
        HF = [hf_mix, hf_peer, hf_conv, hf_peer]
        GN = ["g_mix0", "g_ffn0", "g_mix1", "g_ffn1"]

        H_EVENT = {"n0": 0, "mix": 1, "n1": 2, "n2": 3, "ln": 4, "n3": 5}

        @block.tensor
        def _(pe):
            def norm(n):
                hf = HF[n]
                for k in range(KC):
                    pe.wait_ge(s_sq, 8 * n + k + 1)
                    for a in range(2):
                        m = T.matmul(PA[0][:, a, 0:HALF], ones, hf[:, k, a * HALF:(a + 1) * HALF],
                                     start=(k == 0), stop=(k == KC - 1))
                m.then_inc(s_sum, 1)

            def proj(t, first=False, event=None):
                if first:
                    pe.wait_ge(s_hl, 8 * (H_EVENT[event] + 1))
                    pe.wait_ge(s_hh, 8 * (H_EVENT[event] + 1))
                pe.wait_ge(s_lo, t + 1)
                for k in range(KC):
                    for i, (w, h) in enumerate(((ring_hi, hh), (ring_hi, hl), (ring_lo, hh))):
                        for a in range(2):
                            m = T.matmul(PA[t % 2][:, a, 0:HALF], w[:, t % SLOTS, k * P:(k + 1) * P],
                                         h[:, k, a * HALF:(a + 1) * HALF],
                                         start=(k == 0 and i == 0), stop=(k == KC - 1 and i == 2))
                m.then_inc(s_used, 1)

            def qk_sum(j):
                pe.wait_ge(s_ev, j + 1)
                if j >= 1:
                    pe.wait_ge(s_qroot, j)
                for a in range(2):
                    m = T.matmul(PB[0][:, a, 0:HALF], mcc("blk"), sqz[j % 2][:, a * HALF:(a + 1) * HALF],
                                 start=True, stop=True)
                m.then_inc(s_qsum, 1)

            def qk_rot(j):
                pe.wait_ge(s_qn, j + 1)
                if j >= 1:
                    pe.wait_ge(s_qr, j)
                for a in range(2):
                    m = T.matmul(PB[1][:, a, 0:HALF], mcc("rot"), zq[:, j, a * HALF:(a + 1) * HALF],
                                 start=True, stop=True)
                m.then_inc(s_qrot, 1)

            def kv_tokens():
                pe.wait_ge(s_qr, 5)
                pe.wait_ge(s_ev, 6)
                for b in range(NBLK):
                    T.transpose(PB[0][:, 0, b * P:(b + 1) * P], vT[:, b * P:(b + 1) * P], ident)
                T.transpose(PB[0][:, 1, 0:P], krp[:, NP:NP + P], ident)
                T.transpose(PB[0][0:NS, 1, P:2 * P], krp[:, P + NP:P + NT], ident)
                T.transpose(PB[0][0:NS, 1, 2 * P:3 * P], vT[:, NP:NT], ident).then_inc(s_vt, 1)

            def scores(u):
                blk, j = divmod(u, 4)
                if u >= 2:
                    pe.wait_ge(s_sm, u - 1)
                else:
                    pe.wait_ge(s_vev, 2)
                    pe.wait_ge(s_pad, 4)
                for g in range(2):
                    m = T.matmul(PB[0][:, u % 2, g * 256:(g + 1) * 256], zq[:, j, blk * P:(blk + 1) * P],
                                 krz[:, g, blk * P:blk * P + 256], start=True, stop=True)
                m.then_inc(s_s, 1)

            def p_transpose(u):
                pe.wait_ge(s_p, u + 1)
                if u >= 1:
                    pe.wait_ge(s_pt, u)
                for g in range(2):
                    for b in range(2):
                        m = T.transpose(PB[1][:, 0, (2 * g + b) * P:(2 * g + b + 1) * P],
                                        sm[u % 2][:, g, b * P:(b + 1) * P], ident)
                m.then_inc(s_t, 1)

            def pv(u):
                blk, j = divmod(u, 4)
                pe.wait_ge(s_pt, u + 1)
                if u >= 1:
                    pe.wait_ge(s_oe, u)
                for g in range(2):
                    for b in range(2):
                        m = T.matmul(PB[1][64 * g:64 * g + 64, 1, 0:P],
                                     vtok[:, blk + b, 64 * g:64 * g + 64], pT[u % 2][:, 2 * g + b, :],
                                     start=(b == 0), stop=(b == 1))
                m.then_inc(s_o, 1)

            def decode():
                pe.wait_ge(s_dq, 1)
                pe.wait_ge(s_oe, 16)
                for b in range(SB):
                    T.transpose(PA[0][0:ST, b // 4, (b % 4) * P:(b % 4 + 1) * P],
                                vT[:, NP + ST * b:NP + ST * b + ST], ident)
                for b in range(SB):
                    m = T.matmul(PB[0][32 * (b % 4):32 * (b % 4) + 32, b // 4, 0:WIN + ST],
                                 qbd[:, b, :, :, :].rearrange("p g r t -> p (g r t)"), kcat[:, b, :],
                                 start=True, stop=True)
                m.then_inc(s_ds, 1)
                pe.wait_ge(s_dp, 1)
                for c in range(2):
                    T.transpose(PB[1][:, 0, c * P:(c + 1) * P], pd[:, c, 0:WIN], ident)
                for c in range(2):
                    m = T.transpose(PB[1][0:ST, 0, (2 + c) * P:(3 + c) * P], pd[:, c, WIN:WIN + ST], ident)
                m.then_inc(s_dt, 1)
                pe.wait_ge(s_dpt, 1)
                for b in range(SB):
                    q = slice(32 * (b % 4), 32 * (b % 4) + 32)
                    T.matmul(PB[1][:, 1, 32 * b:32 * b + 32], vcat[:, b, :], pdT[:, b // 4, q],
                             start=True, stop=False)
                    m = T.matmul(PB[1][:, 1, 32 * b:32 * b + 32], vnew[:, b, :], pdN[:, b // 4, q],
                                 start=False, stop=True)
                m.then_inc(s_do, 1)

            def chunk_a(s):
                off, C = CHUNKS[s]
                if s >= 2:
                    pe.wait_ge(s_ki, s - 1)
                for h in range(4):
                    T.transpose(PA[s % 2][0:C, 0, h * P:(h + 1) * P], hK[:, h, off:off + C], ident)
                for h in range(4):
                    m = T.transpose(PA[s % 2][0:C, 1, h * P:(h + 1) * P], gates[:, 12 + h, off:off + C], ident)
                m.then_inc(s_tr, 1)
                if s >= 1:
                    pe.wait_ge(s_am, s)
                for h in range(4):
                    c = h * 16
                    m = T.matmul(PB[0][0:C, 0, c:c + C], hK1[:, h, off:off + C], hQ1[:, h, off:off + C],
                                 start=True, stop=True)
                m.then_inc(s_at, 1)

            def chunk_b(s):
                off, C = CHUNKS[s]
                b = s - NPC
                st = S if b < 0 else Ssm[b % 2]
                pe.wait_ge(s_am, s + 1)
                pe.wait_ge(s_ki, s + 1)
                if b >= 0:
                    pe.wait_ge(s_sl[b % 2], 16 * (b // 2 + 1))
                else:
                    pe.wait_ge(s_S, s + 1)
                if s >= 1:
                    pe.wait_ge(s_oce, s)
                for h in range(4):
                    c = h * 16
                    T.matmul(PB[0][:, 1, c:c + C], st[:, h, :], gates[:, 4 + h, off:off + C],
                             start=True, stop=False)
                    m = T.matmul(PB[0][:, 1, c:c + C], kiT[0:C, s % 2, 1, h, :], am[0:C, s % 2, h, 0:C],
                                 start=False, stop=True)
                m.then_inc(s_oc, 1)
                if s >= 2:
                    pe.wait_ge(s_S, s)
                for h in range(4):
                    m = T.matmul(PB[1][:, s % 2, h * P:(h + 1) * P], kiT[0:C, s % 2, 0, h, :],
                                 kiT[0:C, s % 2, 1, h, :], start=True, stop=True)
                m.then_inc(s_kv, 1)

            def head_sum(h):
                pe.wait_ge(s_hsq, h + 1)
                if h >= 2:
                    pe.wait_ge(s_hr, h - 1)
                for a in range(2):
                    m = T.matmul(PA[h % 2][:, a, 0:HALF], ones, hT1[:, h, a * HALF:(a + 1) * HALF],
                                 start=True, stop=True)
                m.then_inc(s_hs, 1)

            def retrieval(l):
                pe.wait_ge(s_keys, 16 * (l + 1))
                ev0 = N_IN + N_WQ * l
                for i in range(N_WQ + 1):
                    if i < N_WQ:
                        if i >= 2:
                            pe.wait_ge(s_ev, ev0 + i - 1)
                        proj(T_WQ[l] + i, i == 0, "n1" if l == 0 else "n3")
                    if i >= 1:
                        q = i - 1
                        pe.wait_ge(s_ev, ev0 + q + 1)
                        if q >= 2:
                            pe.wait_ge(s_scf, N_WQ * l + q - 1)
                        for n in range(NTILE):
                            m = T.matmul(PB[q % 2][0:ROWS[n], n // 4, (n % 4) * P:(n % 4 + 1) * P],
                                         qh[:, q % 2, n * P:n * P + ROWS[n]], keys[:, q, :],
                                         start=True, stop=True)
                        m.then_inc(s_sc, 1)

            def gate_matrix(l):
                for n in range(NTILE):
                    pe.wait_ge(s_sel, NTILE * l + n + 1)
                    if n == 0:
                        pe.wait_ge(s_scf, N_WQ * (l + 1))
                    else:
                        pe.wait_ge(s_slT, NTILE * l + n)
                    for i in range(3):
                        m = T.transpose(PB[0][:, 0, i * P:i * P + ROWS[n]],
                                        sel[0:ROWS[n], i, :, :].rearrange("p h r -> p (h r)"),
                                        ident[0:ROWS[n], 0:ROWS[n]])
                    m.then_inc(s_selT, 1)
                    for q in range(ROWS[n] // 8):
                        e = (NT // 8) * l + n * 16 + q
                        pe.wait_ge(s_oh, e + 1)
                        if e - (NT // 8) * l >= 2:
                            pe.wait_ge(s_gs, e - 1)
                        for i in range(8):
                            m = T.matmul(PA[e % 2][:, i // 4, (i % 4) * P:(i % 4 + 1) * P],
                                         oh2[:, e % 2, i, :], oh1[:, e % 2, i, :], start=True, stop=True)
                        m.then_inc(s_gm, 1)

            def experts(l):
                t0 = T_EXP[l]
                base_e, base_y = NKEY * l, 8 * NG * l

                def act_in(slot, pair, t, e_free):
                    pe.wait_ge(s_lo, t)
                    pe.wait_ge(s_ga, e_free)
                    for k in range(KC):
                        for i, (w, h) in enumerate(((ring_hi, hh), (ring_hi, hl), (ring_lo, hh))):
                            for a in range(2):
                                m = T.matmul(PA[pair][:, a, 0:HALF], w[:, slot, k * P:(k + 1) * P],
                                             h[:, k, a * HALF:(a + 1) * HALF],
                                             start=(k == 0 and i == 0), stop=(k == KC - 1 and i == 2))
                    m.then_inc(s_used, 1)

                def act_out(slots, par_, g, t):
                    for c in range(KC):
                        if c == 0:
                            pe.wait_ge(s_lo, t)
                            pe.wait_ge(s_ya, base_y + 8 * g)
                        if c >= 2:
                            pe.wait_ge(s_ya, base_y + 8 * g + c - 1)
                        for j in range(GRP):
                            if c == 0:
                                pe.wait_ge(s_wl, base_e + 4 * g + j + 1)
                            ws = j if (j or not par_) else 4
                            for i, (w, h) in enumerate(((ring_hi, wh), (ring_hi, wl), (ring_lo, wh))):
                                for a in range(2):
                                    m = T.matmul(PB[c % 2][:, a, 0:HALF], w[:, slots[j], c * P:(c + 1) * P],
                                                 h[:, ws, a * HALF:(a + 1) * HALF],
                                                 start=(j == 0 and i == 0), stop=(j == GRP - 1 and i == 2))
                                    if c == KC - 1 and i == 2 and a == 1 and j < GRP - 1:
                                        m.then_inc(s_used, 1)
                        if c < KC - 1:
                            m.then_inc(s_y, 1)
                        else:
                            m.then_inc(s_used, 1)

                def group(g, par_, last=False):
                    t = t0 + 1 + 8 * g
                    n_u = 3 if last else 4
                    for j in range(1, n_u + 1):
                        act_in((t0 + j) % SLOTS, j % 2, t + j, base_e + 4 * g + j - 1)
                    sl = [(t0 + 1 + n_u + j) % SLOTS for j in range(GRP)]
                    act_out(sl, par_, g, t + n_u + GRP)

                pe.wait_ge(s_gs, (NT // 8) * (l + 1))
                pe.wait_ge(s_hl, 8)
                act_in(t0 % SLOTS, 0, t0 + 1, base_e)
                with pe.Fori(0, NG // 2 - 1) as i:
                    group(2 * i, 0)
                    group(2 * i + 1, 1)
                group(NG - 2, 0)
                group(NG - 1, 1, True)

            norm(0)
            for m in range(N_IN):
                if m >= 2:
                    pe.wait_ge(s_ev, m - 1)
                proj(T_IN + m, m == 0, "n0")
                if m == 0:
                    pe.wait_ge(s_mc, 16)
                if 1 <= m <= 5:
                    qk_sum(m - 1)
                if 2 <= m <= 6:
                    qk_rot(m - 2)
                if m == 7:
                    kv_tokens()
                if m >= 8:
                    for u in (2 * (m - 8), 2 * (m - 8) + 1):
                        if u < 16:
                            scores(u)
                        if 0 <= u - 2 < 16:
                            p_transpose(u - 2)
                        if 0 <= u - 3 < 16:
                            pv(u - 3)
            pe.wait_ge(s_ev, N_IN)
            decode()
            pe.wait_ge(s_h, 1)
            pe.wait_ge(s_dend, 2)
            for s in range(NCH + 1):
                if s < NCH:
                    chunk_a(s)
                if s >= 1:
                    chunk_b(s - 1)
            for h in range(4):
                head_sum(h)
            for i in range(N_OUT):
                if i >= 2:
                    pe.wait_ge(s_res, i - 1)
                proj(T_OUT + i, i == 0, "mix")
            norm(1)
            retrieval(0)
            gate_matrix(0)
            experts(0)
            norm(2)
            for i in range(16):
                if i >= 2:
                    if i % 2 == 0:
                        pe.wait_ge(s_u, 3 * (i // 2))
                    else:
                        pe.wait_ge(s_sg, i // 2)
                proj(T_PW1 + i, i == 0, "n2")
            for k in range(KC):
                pe.wait_ge(s_cv, k + 1)
                for a in range(2):
                    m = T.matmul(PB[0][:, a, 0:HALF], ones, cv[:, k, a * HALF:(a + 1) * HALF],
                                 start=(k == 0), stop=(k == KC - 1))
            m.then_inc(s_ms, 1)
            for k in range(KC):
                pe.wait_ge(s_csq, k + 1)
                for a in range(2):
                    m = T.matmul(PB[1][:, a, 0:HALF], ones, hf_conv[:, k, a * HALF:(a + 1) * HALF],
                                 start=(k == 0), stop=(k == KC - 1))
            m.then_inc(s_vs, 1)
            for i in range(KC):
                if i >= 2:
                    pe.wait_ge(s_res, 8 + i - 1)
                proj(T_PW2 + i, i == 0, "ln")
            norm(3)
            retrieval(1)
            gate_matrix(1)
            experts(1)

        @block.scalar
        def _(act):
            ch = Chain(act, s_a)

            def hi(t):
                act.wait_ge(s_raw[t % 2], 16 * (t // 2 + 1))
                if t >= SLOTS:
                    act.wait_ge(s_used, t - SLOTS + 1)
                A.activation(ring_hi[:, t % SLOTS, :], raw[t % 2][:], ACT.Copy).then_inc(s_hi, 1)

            def hi_parts(src, ev, n=KC):
                for k in range(n):
                    A.activation(hh[:, k, :], src(k), ACT.Copy).then_inc(s_hh, 1)

            def norm(n):
                wait_x(act, n)
                for k in range(KC):
                    A.activation(HF[n][:, k, :], xt[:, k, :], ACT.Square).then_inc(s_sq, 1)
                act.wait_ge(s_sum, n + 1)
                A.activation(tok2(root[:, :]), both(PA[0]), ACT.Sqrt, bias=eps, scale=1.0 / D)\
                    .then_inc(s_root, 1)
                for k in range(KC):
                    act.wait_ge(s_hf, 8 * n + k + 1)
                    A.activation(hh[:, k, :], HF[n][:, k, :], ACT.Copy).then_inc(s_hh, 1)

            def evac(t, out, fn=ACT.Copy):
                act.wait_ge(s_used, t + 1)
                A.activation(tok2(out), both(PA[t % 2]), fn).then_inc(s_ev, 1)

            def attn_exp(u):
                b = u % 2
                act.wait_ge(s_nm, u + 1)
                for g in range(2):
                    ch.done(A.activation(sm[b][:, g, :], sm[b][:, g, :], ACT.Exp, bias=st8[:, b, 2 + g:3 + g],
                                         accum_out=st8[:, b, 6 + g:7 + g]))
                A.activation(st8[:, b, 8:10], st8[:, b, 4:6], ACT.Exp).then_inc(s_pe, 1)

            def attn_pT(u):
                act.wait_ge(s_t, u + 1)
                if u >= 2:
                    act.wait_ge(s_o, u - 1)
                A.activation(pT[u % 2], PB[1][:, 0, :].rearrange("p (a q) -> p a q", a=4), ACT.Copy)\
                    .then_inc(s_pt, 1)

            def attn_out(u):
                blk, j = divmod(u, 4)
                act.wait_ge(s_o, u + 1)
                A.activation(zq[:, j, blk * P:(blk + 1) * P], PB[1][:, 1, 0:P], ACT.Copy)\
                    .then_inc(s_oe, 1)

            def retrieval(l):
                norm(1 if l == 0 else 3)
                for i in range(N_WQ):
                    t = T_WQ[l] + i
                    if i >= 2:
                        act.wait_ge(s_sc, N_WQ * l + i - 1)
                    if t + LOOK < T_WQ[l] + N_WQ:
                        hi(t + LOOK)
                    evac(t, qh[:, i % 2, :])
                for n in range(NTILE):
                    R = ROWS[n]
                    act.wait_ge(s_gx, NTILE * l + n + 1)
                    A.activation(sel[0:R, 2, :, :], r16[0:R, :, :], ACT.Exp).then_inc(s_ge, 1)
                    act.wait_ge(s_selT, NTILE * l + n + 1)
                    A.activation(slT[:, :, n * P:n * P + R],
                                 PB[0][:, 0, 0:3 * P].rearrange("p (i r) -> p i r", i=3)[:, :, 0:R], ACT.Copy)\
                        .then_inc(s_slT, 1)
                    if n >= 1:
                        act.wait_ge(s_gw, 64 * (NTILE * l + n))
                    for q in range(R // 8):
                        e = (NT // 8) * l + n * 16 + q
                        act.wait_ge(s_gm, e + 1)
                        A.activation(stage[:, :, 8 * q:8 * q + 8].rearrange("p k t -> p t k"),
                                     PA[e % 2][:, :, :].rearrange("p a (t k) -> p (a t) k", t=4), ACT.Copy)\
                            .then_inc(s_gs, 1)
                    act.wait_ge(s_gs, (NT // 8) * l + n * 16 + R // 8)
                    for i in range(4):
                        act.dma_start(gdram[l, 32 * i:32 * i + 32, :, n * P:n * P + R].rearrange("k p t -> p k t"),
                                      stage[:, 32 * i:32 * i + 32, 0:R]).then_inc(s_gw, 16)
                act.wait_ge(s_gw, 64 * NTILE * (l + 1))

            def experts(l):
                t0, b_e = T_EXP[l], NKEY * l

                def load_gate(slot, e):
                    act.dma_start(gt[:, slot, :], gdram[l, bass.ds(e, 1)].rearrange("a p n -> (a p) n")
                                  if not isinstance(e, int) else gdram[l, e]).then_inc(s_gld[slot], 16)

                def hi_at(slot, buf, n_loaded, used):
                    act.wait_ge(s_raw[buf], n_loaded)
                    act.wait_ge(s_used, used)
                    A.activation(ring_hi[:, slot, :], raw[buf][:], ACT.Copy).then_inc(s_hi, 1)

                def hi_rel(t, k):
                    u = t0 + 1 + k
                    hi_at(u % SLOTS, u % 2, loads(t, k), t + k - SLOTS + 1)

                def loads(t, k):
                    odd = (t0 + 1 + k) % 2
                    return (t + (k - odd)) * 8 + 16

                def gelu(e, par_e, t_used):
                    act.wait_ge(s_used, t_used)
                    A.activation(tok2(ga[:, par_e, :]), both(PA[par_e]), ACT.Gelu).then_inc(s_ga, 1)

                def split(e, slot, ws, load=True):
                    act.wait_ge(s_w, b_e + e + 1)
                    if load:
                        load_gate(slot, e + GRP)
                    A.activation(wh[:, ws, :], ga[:, slot % 2, :], ACT.Copy).then_inc(s_wh, 1)

                def group(g, par_, last=False):
                    t = t0 + 1 + 8 * g
                    n_u = 3 if last else 4
                    ahead = [k for k in range(n_u, n_u + 4)]
                    hi_rel(t, ahead[0])
                    hi_rel(t, ahead[1])
                    for j in range(1, n_u + 1):
                        e = 4 * g + j
                        act.wait_ge(s_wl, b_e + e - 1)
                        gelu(e, j % 2, t + j)
                        if j == 1:
                            hi_rel(t, ahead[2])
                        split(e, j % 4, (j % 4) if j % 4 else (0 if par_ else 4), not last)
                        if j == 1:
                            hi_rel(t, ahead[3])
                        if not last and j >= 2:
                            for k in {2: (8,), 3: (9,), 4: (10, 11)}[j]:
                                hi_rel(t, k)

                for i in range(GRP):
                    load_gate(i, i)
                for k in range(LOOK + 1):
                    hi(t0 + k)
                gelu(0, 0, t0 + 1)
                split(0, 0, 0)
                with act.Fori(0, NG // 2 - 1) as i:
                    for v in range(2):
                        g = 2 * i + v
                        group(g, v)
                t = t0 + 1 + 8 * (NG - 2)
                hi_rel(t, 4)
                hi_rel(t, 5)
                for j in range(1, 5):
                    e = 4 * (NG - 2) + j
                    act.wait_ge(s_wl, b_e + e - 1)
                    gelu(e, j % 2, t + j)
                    if j == 1:
                        hi_rel(t, 6)
                    split(e, j % 4, (j % 4) if j < 4 else 4, e + GRP < NKEY)
                    if j == 1:
                        hi_rel(t, 7)
                    if j >= 2:
                        hi_rel(t, 6 + j)
                group(NG - 1, 1, True)

            act.dma_start(par[:], params).then_inc(s_par, 16)
            act.dma_start(con[:], consts).then_inc(s_par, 16)
            act.dma_start(mc[:], mconsts).then_inc(s_mc, 16)
            act.dma_start(kwin_s[:, 0:WIN - ST, :], kvcache_n[0, :, ST:WIN, :]).then_inc(s_out, 16)
            act.dma_start(vwin_s[:, 0:WIN - ST, :], kvcache_n[1, :, ST:WIN, :]).then_inc(s_out, 16)
            for t in range(LOOK):
                hi(t)
            act.wait_ge(s_par, 32)
            act.wait_ge(s_eps, 1)
            norm(0)
            n_dma = 32
            for m in range(N_IN):
                if m + LOOK < N_IN:
                    hi(m + LOOK)
                if m < 5:
                    act.wait_ge(s_used, m + 1)
                    if m >= 2:
                        act.wait_ge(s_qsum, m - 1)
                    ch.done(A.activation(tok2(zq[:, m, :]), both(PA[m % 2]), ACT.Copy))
                    A.activation(tok2(sqz[m % 2]), both(PA[m % 2]), ACT.Square).then_inc(s_ev, 1)
                elif m == 5:
                    evac(m, vT[:, :])
                elif m < 10:
                    evac(m, gates[:, m - 6, :])
                elif m < 18:
                    evac(m, gates[:, m - 6, :], ACT.Silu)
                else:
                    evac(m, gates[:, m - 6, :])
                if 1 <= m <= 5:
                    act.wait_ge(s_qsum, m)
                    if m >= 2:
                        act.wait_ge(s_qn, m - 1)
                    A.activation(tok2(rt), both(PB[0]), ACT.Sqrt, bias=eps, scale=1.0 / HD).then_inc(s_qroot, 1)
                if m == 7:
                    act.wait_ge(s_vt, 1)
                    A.activation(vtok[:, 1:5, :], PB[0][:, 0, :].rearrange("p (b f) -> p b f", b=4), ACT.Copy)\
                        .then_inc(s_vev, 1)
                    ch.done(A.activation(kvo[:, 0, :], PB[0][:, 1, 0:P], ACT.Copy))
                    A.activation(kvo[0:NS, 1:3, :],
                                 PB[0][0:NS, 1, P:3 * P].rearrange("p (i f) -> p i f", i=2), ACT.Copy)\
                        .then_inc(s_vev, 1)
                    act.wait_ge(s_vev, 2)
                    ch.sync()
                    act.dma_start(kwin_p, kvo[:, 0, :]).then_inc(s_out, 16)
                    act.dma_start(vwin_p, vtok[:, 4, :]).then_inc(s_out, 16)
                    act.dma_start(kwin_s[:, WIN - ST:WIN, :], kvo[0:NS, 1, :]).then_inc(s_out, 16)
                    act.dma_start(vwin_s[:, WIN - ST:WIN, :], kvo[0:NS, 2, :]).then_inc(s_out, 16)
                    n_dma += 64
                if m >= 8:
                    for u in (2 * (m - 8), 2 * (m - 8) + 1):
                        if u < 16:
                            attn_exp(u)
                        if 0 <= u - 2 < 16:
                            attn_pT(u - 2)
                        if 0 <= u - 3 < 16:
                            attn_out(u - 3)

            act.wait_ge(s_ev, N_IN)
            act.wait_ge(s_used, N_IN)
            A.activation(hT1[:, :, :], gates[:, 0:4, :], ACT.Sigmoid).then_inc(s_ha, 1)
            A.activation(hK[:, :, :], gates[:, 0:4, :], ACT.Sigmoid, scale=-1.0).then_inc(s_ha, 1)
            act.wait_ge(s_lbx, 2)
            A.activation(small[:, 28:36], small[:, 16:24], ACT.Exp).then_inc(s_lb, 1)
            act.wait_ge(s_ds, 1)
            A.activation(vnew[:, :, :], PA[0][0:ST, :, :].rearrange("p a (b f) -> p (a b) f", b=4), ACT.Copy)\
                .then_inc(s_dv, 1)
            act.wait_ge(s_dnm, 1)
            for c in range(2):
                ch.done(A.activation(pd[:, c, :], pd[:, c, :], ACT.Exp, bias=st8[:, 0, 2 + c:3 + c],
                                     accum_out=st8[:, 0, 6 + c:7 + c]))
            A.activation(st8[:, 0, 8:10], st8[:, 0, 4:6], ACT.Exp).then_inc(s_de, 1)
            act.wait_ge(s_dt, 1)
            ch.done(A.activation(pdT[:, :, :], PB[1][:, 0, 0:2 * P].rearrange("p (c q) -> p c q", c=2), ACT.Copy))
            ch.sync()
            act.wait_ge(s_dv, 1)
            A.activation(pdN[:, :, :], PB[1][0:ST, 0, 2 * P:4 * P].rearrange("p (c q) -> p c q", c=2), ACT.Copy)\
                .then_inc(s_dpt, 1)
            act.wait_ge(s_do, 1)
            for g in range(2):
                r = slice(64 * g, 64 * g + 64)
                o = PB[1][r, 1, 0:256].rearrange("p (b g r t) -> p g r b t", b=8, g=2, r=4)[:, g]
                A.activation(zq[r, 0:4, NP:NT].rearrange("p r (b t) -> p r b t", b=8), o, ACT.Copy)\
                    .then_inc(s_dend, 1)
            act.wait_ge(s_hd, 1)
            A.activation(hT1[:, :, :], hT1[:, :, :], ACT.Ln).then_inc(s_ha, 1)
            act.wait_ge(s_hd, 2)
            A.activation(hT2[:, :, :], hT1[:, :, :], ACT.Exp).then_inc(s_ha, 1)
            act.wait_ge(s_hd, 3)
            A.activation(hT2[:, :, :], hT1[:, :, :], ACT.Exp, scale=-1.0).then_inc(s_ha, 1)
            act.wait_ge(s_hd, 4)
            A.activation(hT2[:, :, :], gates[:, 0:4, :], ACT.Exp).then_inc(s_ha, 1)
            act.wait_ge(s_hd, 5)
            A.activation(hT2[:, :, :], hT1[:, :, :], ACT.Exp).then_inc(s_ha, 1)
            ch.done(A.activation(hD[:, :, 0:NPC],
                                 gates[:, 0:4, 0:NP].rearrange("p h (c t) -> p h c t", t=16)[:, :, :, 15], ACT.Exp))
            ch.done(A.activation(hD[:, :, NPC:NCH],
                                 gates[:, 0:4, NP:NT].rearrange("p h (c t) -> p h c t", t=ST)[:, :, :, ST - 1],
                                 ACT.Exp))
            ch.sync()
            A.activation(small[:, 1:2], small[:, 0:1], ACT.Copy).then_inc(s_ha, 1)
            act.wait_ge(s_dend, 2)
            for s in range(NCH + 1):
                if s < NCH:
                    off, C = CHUNKS[s]
                    act.wait_ge(s_tr, s + 1)
                    if s >= 2:
                        act.wait_ge(s_kv, s - 1)
                    A.activation(kiT[0:C, s % 2, :, :, :],
                                 PA[s % 2][0:C, :, :].rearrange("p a (h f) -> p a h f", h=4), ACT.Copy)\
                        .then_inc(s_ki, 1)
                if s >= 1:
                    off, C = CHUNKS[s - 1]
                    act.wait_ge(s_oc, s)
                    A.activation(hO[:, :, off:off + C],
                                 PB[0][:, 1, 0:64].rearrange("p (h t) -> p h t", h=4)[:, :, 0:C], ACT.Copy)\
                        .then_inc(s_oce, 1)
            act.wait_ge(s_oce, NCH)
            for h in range(4):
                A.activation(hT1[:, h, :], hO[:, h, :], ACT.Square).then_inc(s_hsq, 1)
            for h in range(4):
                act.wait_ge(s_hs, h + 1)
                A.activation(tok2(hT2[:, h, :]), both(PA[h % 2]), ACT.Sqrt, bias=eps, scale=1.0 / P)\
                    .then_inc(s_hr, 1)
            for h in range(4):
                A.activation(hh[:, h, :], zq[:, h, :], ACT.Copy).then_inc(s_hh, 1)
            for h in range(4):
                act.wait_ge(s_mixf, h + 1)
                A.activation(hh[:, 4 + h, :], hO[:, h, :], ACT.Copy).then_inc(s_hh, 1)
            act.wait_ge(s_hl, 16)
            for t in range(T_OUT, T_OUT + LOOK):
                hi(t)
            for i in range(LOOK, N_OUT):
                hi(T_OUT + i)
            act.wait_ge(s_out, 16 * 6)
            for t in range(T_WQ[0], T_WQ[0] + LOOK):
                hi(t)
            retrieval(0)
            experts(0)
            for t in range(T_PW1, T_PW1 + LOOK):
                hi(t)
            norm(2)
            for i in range(16):
                if T_PW1 + LOOK + i < T_PW2 + KC:
                    hi(T_PW1 + LOOK + i)
                if i % 2:
                    m = i // 2
                    act.wait_ge(s_used, T_PW1 + i + 1)
                    if m >= 2:
                        act.wait_ge(s_u, 3 * (m - 1))
                    A.activation(tok2(sg[:, m % 2, :]), both(PA[(T_PW1 + i) % 2]), ACT.Sigmoid,
                                 bias=pc("b1", 8 + m)).then_inc(s_sg, 1)
            act.wait_ge(s_u, 24)
            act.dma_start(cb_p.rearrange("(k p) n -> p k n", p=P), up[:, :, NP:NP + CW - 1]).then_inc(s_out, 16)
            for k in range(KC):
                act.dma_start(cb_s[k * P:(k + 1) * P], us[:, k, :, ST:ST + CW - 1]).then_inc(s_out, 16)
            for k in range(KC):
                act.wait_ge(s_cen, k + 1)
                A.activation(hf_conv[:, k, :], cv[:, k, :], ACT.Square).then_inc(s_csq, 1)
            act.wait_ge(s_vs, 1)
            A.activation(tok2(root[:, :]), both(PB[1]), ACT.Sqrt, bias=eps, scale=1.0 / D).then_inc(s_cr, 1)
            for k in range(KC):
                act.wait_ge(s_ln, k + 1)
                A.activation(cv[:, k, :], cv[:, k, :], ACT.Silu, bias=pc("lnb", k)).then_inc(s_si, 1)
            for k in range(KC):
                act.wait_ge(s_si, k + 1)
                A.activation(hh[:, k, :], cv[:, k, :], ACT.Copy).then_inc(s_hh, 1)
            for t in range(T_PW1 + LOOK + 16, T_PW2 + KC):
                hi(t)
            act.wait_ge(s_out, 16 * 15)
            for t in range(T_WQ[1], T_WQ[1] + LOOK):
                hi(t)
            retrieval(1)
            experts(1)
            act.wait_ge(s_ya, 16 * NG)
            act.dma_start(yT.rearrange("(k p) n -> p k n", p=P), xt[:]).then_inc(s_out, 16)
            act.wait_ge(s_out, 16 * (2 + 4 + 9 + 1))

        @block.vector
        def _(dve):
            ch = Chain(dve, s_v)

            def norm(n):
                dve.wait_ge(s_root, n + 1)
                ch.step(V.reciprocal(root[:, :], root[:, :]))
                for k in range(KC):
                    V.scalar_tensor_tensor(out=HF[n][:, k, :], in0=xt[:, k, :], scalar=pc(GN[n], k),
                                           in1=root[:, :], op0=ALU.mult, op1=ALU.mult).then_inc(s_hf, 1)
                lo_parts([HF[n][:, k, :] for k in range(KC)], ["n0", "n1", "n2", "n3"][n])

            def lo_parts(src, event, k0=0):
                for k, a in enumerate(src):
                    dve.wait_ge(s_hh, 8 * H_EVENT[event] + k0 + k + 1)
                    V.tensor_tensor(hl[:, k0 + k, :], a, hh[:, k0 + k, :].bitcast(F32), ALU.subtract)\
                        .then_inc(s_hl, 1)

            def softmax_a(u):
                b = u % 2
                blk, j = divmod(u, 4)
                dve.wait_ge(s_s, u + 1)
                if u >= 2:
                    dve.wait_ge(s_t, u - 1)
                mask = mcc("band0" if blk == 0 else "band")
                V.scalar_tensor_tensor(out=sm[b], in0=PB[0][:, b, :].rearrange("p (g k) -> p g k", g=2),
                                       scalar=SCALE, in1=mask.unsqueeze(1).to_broadcast([P, 2, 256]),
                                       op0=ALU.mult, op1=ALU.add).then_inc(s_sm, 1)
                dve.wait_ge(s_sm, u + 1)
                ch.step(V.tensor_reduce(st8[:, b, 0:2], sm[b], X, ALU.max))
                ch.step(V.tensor_tensor(st8[:, b, 0:2], st8[:, b, 0:2], pc("sink", 2 * j, 2), ALU.max))
                ch.step(V.tensor_scalar(st8[:, b, 2:4], st8[:, b, 0:2], -1.0, None, ALU.mult))
                V.tensor_tensor(st8[:, b, 4:6], pc("sink", 2 * j, 2), st8[:, b, 2:4], ALU.add).then_inc(s_nm, 1)

            def softmax_b(u):
                b = u % 2
                dve.wait_ge(s_pe, u + 1)
                ch.step(V.tensor_tensor(st8[:, b, 10:12], st8[:, b, 6:8], st8[:, b, 8:10], ALU.add))
                ch.step(V.reciprocal(st8[:, b, 12:14], st8[:, b, 10:12]))
                ch.step(V.tensor_scalar(sm[b][:, 0, :], sm[b][:, 0, :], st8[:, b, 12:13], None, ALU.mult))
                V.tensor_scalar(sm[b][:, 1, :], sm[b][:, 1, :], st8[:, b, 13:14], None, ALU.mult).then_inc(s_p, 1)

            def retrieval(l):
                norm(1 if l == 0 else 3)
                for q in range(N_WQ):
                    dve.wait_ge(s_sc, N_WQ * l + q + 1)
                    src = [PB[q % 2][0:ROWS[n], n // 4, (n % 4) * P:(n % 4 + 1) * P] for n in range(NTILE)]
                    val = [sv[0:ROWS[n], n, q, :] for n in range(NTILE)]
                    idx = [si[0:ROWS[n], n, q, :] for n in range(NTILE)]
                    tmp = [sc2[0:ROWS[n], n, :] for n in range(NTILE)]
                    for n in range(NTILE):
                        ch.done(V.max(val[n][:, 0:8], src[n]))
                    ch.sync()
                    for n in range(NTILE):
                        ch.done(V.max_index(idx[n][:, 0:8], val[n][:, 0:8], src[n]))
                    for n in range(NTILE):
                        m = V.match_replace(out=tmp[n], in_to_replace=val[n][:, 0:8], in_values=src[n],
                                            imm_value=-3e38)
                        if n < NTILE - 1:
                            ch.done(m)
                    m.then_inc(s_scf, 1)
                    ch.sync()
                    dve.wait_ge(s_scf, N_WQ * l + q + 1)
                    for n in range(NTILE):
                        ch.done(V.max(val[n][:, 8:16], tmp[n]))
                    ch.sync()
                    for n in range(NTILE):
                        ch.done(V.max_index(idx[n][:, 8:16], val[n][:, 8:16], tmp[n]))
                    ch.sync()
                for n in range(NTILE):
                    select(l, n)
                    onehots(l, n)

            def select(l, n):
                R = ROWS[n]
                val = sv[0:R, n, :, :].rearrange("p (h s) k -> p h s k", s=2)
                ch.done(V.tensor_copy(sif[0:R, :, :], si[0:R, n, :, :]))
                for a in range(8):
                    w = CAND_W[a]
                    ch.done(V.tensor_tensor(cand[0:R, :, CAND_AT[a]:CAND_AT[a] + w],
                                            val[:, :, 1, 0:w],
                                            val[:, :, 0, a:a + 1].to_broadcast([R, 8, w]), ALU.add))
                ch.done(V.tensor_tensor(cand[0:R, :, CAND_AT[8]:NCAND], val[:, :, 0, 8:16],
                                        val[:, :, 1, 0:1].to_broadcast([R, 8, 8]), ALU.add))
                ch.sync()
                for h in range(8):
                    ch.done(V.max(fv[0:R, h, 0:8], cand[0:R, h, :]))
                ch.sync()
                for h in range(8):
                    ch.done(V.max_index(fi[0:R, h, 0:8], fv[0:R, h, 0:8], cand[0:R, h, :]))
                    ch.done(V.match_replace(out=cand2[0:R, h, :], in_to_replace=fv[0:R, h, 0:8],
                                            in_values=cand[0:R, h, :], imm_value=-3e38))
                ch.sync()
                for h in range(8):
                    ch.done(V.max(fv[0:R, h, 8:16], cand2[0:R, h, :]))
                ch.sync()
                for h in range(8):
                    ch.done(V.max_index(fi[0:R, h, 8:16], fv[0:R, h, 8:16], cand2[0:R, h, :]))
                if n >= 1 or l >= 1:
                    dve.wait_ge(s_ge, NTILE * l + n)
                    dve.wait_ge(s_selT, NTILE * l + n)
                V.tensor_tensor(r16[0:R, :, :], fv[0:R, :, :], fv[0:R, :, 0:1].to_broadcast([R, 8, 16]),
                                ALU.subtract).then_inc(s_gx, 1)
                ch.sync()
                ch.done(V.tensor_copy(pos[0:R, :, :], fi[0:R, :, :]))
                sidx = sif[0:R, :, :].rearrange("p (h s) k -> p h s k", s=2)
                ch.done(V.tensor_tensor(dsi[0:R, :, :], sidx[:, :, 0, 1:16], sidx[:, :, 0, 0:15], ALU.subtract))
                ch.sync()
                start, dstart = cc("start"), cc("dstart")
                iota16 = iota[0:R, 0:16]
                for f in range(2):
                    hs = slice(4 * f, 4 * f + 4)
                    g15, t15 = ge[0:R, :, :, 0:15], tm[0:R, :, :, 0:15]
                    s4 = [R, 4, 16, 15]
                    for h in range(4):
                        ch.done(V.tensor_tensor(ge[0:R, h, :, 0:15],
                                                pos[0:R, 4 * f + h, :].unsqueeze(2).to_broadcast([R, 16, 15]),
                                                start[0:R, :].unsqueeze(1).to_broadcast([R, 16, 15]), ALU.is_ge))
                    ch.sync()
                    for h in range(4):
                        ch.done(V.tensor_tensor(tm[0:R, h, :, 0:15], ge[0:R, h, :, 0:15],
                                                dsi[0:R, 4 * f + h, :].unsqueeze(1).to_broadcast([R, 16, 15]),
                                                ALU.mult))
                    ch.sync()
                    ch.step(V.tensor_reduce(sel[0:R, 0, hs, :], t15, X, ALU.add))
                    for h in range(4):
                        ch.done(V.tensor_tensor(tm[0:R, h, :, 0:15], ge[0:R, h, :, 0:15],
                                                dstart[0:R, :].unsqueeze(1).to_broadcast([R, 16, 15]), ALU.mult))
                    ch.sync()
                    ch.step(V.tensor_reduce(sel[0:R, 1, hs, :], t15, X, ALU.add))
                    ch.step(V.tensor_tensor(pos[0:R, hs, :], pos[0:R, hs, :], sel[0:R, 1, hs, :], ALU.subtract))
                    for h in range(4):
                        ch.done(V.tensor_tensor(ge[0:R, h, :, :],
                                                pos[0:R, 4 * f + h, :].unsqueeze(2).to_broadcast([R, 16, 16]),
                                                iota16.unsqueeze(1).to_broadcast([R, 16, 16]), ALU.is_equal))
                    ch.sync()
                    for h in range(4):
                        ch.done(V.tensor_tensor(tm[0:R, h, :, :], ge[0:R, h, :, :],
                                                sidx[:, 4 * f + h, 1, :].unsqueeze(1).to_broadcast([R, 16, 16]),
                                                ALU.mult))
                    ch.sync()
                    ch.step(V.tensor_reduce(sel[0:R, 1, hs, :], tm[0:R, :, :, :], X, ALU.add))
                ch.done(V.tensor_tensor(sel[0:R, 0, :, :], sel[0:R, 0, :, :],
                                        sidx[:, :, 0, 0:1].to_broadcast([R, 8, 16]), ALU.add))
                dve.wait_ge(s_ge, NTILE * l + n + 1)
                ch.step(V.tensor_reduce(r8[0:R, 0, :], sel[0:R, 2, :, :], X, ALU.add))
                ch.step(V.reciprocal(r8[0:R, 1, :], r8[0:R, 0, :]))
                V.tensor_tensor(sel[0:R, 2, :, :], sel[0:R, 2, :, :],
                                r8[0:R, 1, :].unsqueeze(2).to_broadcast([R, 8, 16]), ALU.mult).then_inc(s_sel, 1)

            def onehots(l, n):
                dve.wait_ge(s_slT, NTILE * l + n + 1)
                for q in range(ROWS[n] // 8):
                    e = (NT // 8) * l + n * 16 + q
                    t = n * P + 8 * q
                    if n * 16 + q >= 2:
                        dve.wait_ge(s_gm, e - 1)
                    (V.tensor_tensor(oh2[:, e % 2, :, :], iota.unsqueeze(1).to_broadcast([P, 8, P]),
                                            slT[:, 1, t:t + 8].unsqueeze(2).to_broadcast([P, 8, P]), ALU.is_equal))
                    for i in range(8):
                        m = V.tensor_scalar(oh1[:, e % 2, i, :], iota, slT[:, 0, t + i:t + i + 1],
                                            slT[:, 2, t + i:t + i + 1], ALU.is_equal, ALU.mult)
                    m.then_inc(s_oh, 1)

            def experts(l):
                t0, b_e = T_EXP[l], NKEY * l

                def gate(e, par_e, slot, n_loads, ws):
                    dve.wait_ge(s_ga, b_e + e + 1)
                    dve.wait_ge(s_gld[slot], n_loads)
                    V.tensor_tensor(ga[:, par_e, :], ga[:, par_e, :], gt[:, slot, :], ALU.mult).then_inc(s_w, 1)
                    dve.wait_ge(s_wh, b_e + e + 1)
                    V.tensor_tensor(wl[:, ws, :], ga[:, par_e, :], wh[:, ws, :].bitcast(F32), ALU.subtract)\
                        .then_inc(s_wl, 1)

                def group(g, par_, last=False):
                    t = t0 + 1 + 8 * g
                    n_u = 3 if last else 4
                    for j in range(1, n_u + 1):
                        gg = g if j < 4 else g + 1
                        gate(4 * g + j, j % 2, j % 4, 16 * (NG * l + 1) + 16 * gg,
                             j % 4 if j < 4 else (0 if par_ else 4))
                    for c in range(KC):
                        if c < KC - 1:
                            dve.wait_ge(s_y, (KC - 1) * (NG * l) + (KC - 1) * g + c + 1)
                        else:
                            dve.wait_ge(s_used, t + n_u + GRP)
                        V.tensor_tensor(tok2(xt[:, c, :]), tok2(xt[:, c, :]), both(PB[c % 2]), ALU.add)\
                            .then_inc(s_ya, 1)

                gate(0, 0, 0, 16 * (NG * l + 1), 0)
                with dve.Fori(0, NG // 2 - 1) as i:
                    group(2 * i, 0)
                    group(2 * i + 1, 1)
                group(NG - 2, 0)
                group(NG - 1, 1, True)

            V.memset(small[:], 0.0).then_inc(s_v, 1)
            ch.n += 1
            ch.sync()
            V.memset(small[:, 0:1], EPS).then_inc(s_eps, 1)
            V.memset(krp[:, 0:P], 0.0).then_inc(s_pad, 1)
            ch.step(V.memset(krz[:, :, :], 0.0))
            V.memset(vtok[:, 0, :], 0.0).then_inc(s_pad, 1)
            dve.wait_ge(s_par, 32)
            dve.wait_ge(s_x, 16)
            norm(0)
            dve.wait_ge(s_mc, 16)
            for m in range(1, 7):
                if m <= 5:
                    j = m - 1
                    dve.wait_ge(s_qroot, j + 1)
                    ch.step(V.reciprocal(rt, rt))
                    V.scalar_tensor_tensor(out=zq[:, j, :], in0=zq[:, j, :], scalar=pc("gq" if j < 4 else "gk"),
                                           in1=rt, op0=ALU.mult, op1=ALU.mult).then_inc(s_qn, 1)
                if m >= 2:
                    j = m - 2
                    dve.wait_ge(s_qrot, j + 1)
                    ch.done(V.tensor_tensor(tok2(rt2), both(PB[1]), tok2(mcc("sin")), ALU.mult))
                    ch.step(V.tensor_tensor(zq[:, j, :], zq[:, j, :], mcc("cos"), ALU.mult))
                    out = zq[:, j, :] if j < 4 else krp[:, P:P + NT]
                    V.tensor_tensor(out, zq[:, j, :], rt2, ALU.add).then_inc(s_qr, 1)
            dve.wait_ge(s_qr, 5)
            for g in range(2):
                r = slice(64 * g, 64 * g + 64)
                V.tensor_copy(krz[r, g, P:P + NT], krp[r, P:P + NT]).then_inc(s_pad, 1)
            for u in range(17):
                if u < 16:
                    softmax_a(u)
                if u >= 1:
                    softmax_b(u - 1)
            lb = small[:, 8:12]
            oml = small[:, 12:16]
            ch.step(V.tensor_tensor(small[:, 24:28], pc("lb1", 0, 4), pc("lb0", 0, 4), ALU.max))
            V.tensor_tensor(small[:, 16:20], pc("lb0", 0, 4), small[:, 24:28], ALU.subtract).then_inc(s_lbx, 1)
            V.tensor_tensor(small[:, 20:24], pc("lb1", 0, 4), small[:, 24:28], ALU.subtract).then_inc(s_lbx, 1)
            dve.wait_ge(s_used, N_IN)
            dve.wait_ge(s_dload, 32)
            ch.step(V.memset(qbd[:, :, :, :, :], 0.0))
            ch.done(V.tensor_copy(kcat[:, :, WIN:WIN + ST], krp[:, P + NP:P + NT].rearrange("p (b t) -> p b t", b=SB)))
            for g in range(2):
                r = slice(64 * g, 64 * g + 64)
                for j in range(4):
                    ch.done(V.tensor_copy(qbd[r, :, g, j, :], zq[r, j, NP:NT].rearrange("p (b t) -> p b t", b=SB)))
            ch.sync()
            V.memset(small[:, 2:3], 0.0).then_inc(s_dq, 1)
            dve.wait_ge(s_ds, 1)
            ch.step(V.scalar_tensor_tensor(out=pd[:, :, :], in0=PB[0][:, :, 0:WIN + ST], scalar=SCALE,
                                           in1=mcc("dec").unsqueeze(1).to_broadcast([P, 2, WIN + ST]),
                                           op0=ALU.mult, op1=ALU.add))
            st = st8[:, 0, :]
            ch.step(V.tensor_reduce(st[:, 0:2], pd[:, :, :], X, ALU.max))
            ch.step(V.tensor_scalar(st[:, 0:2], st[:, 0:2], pc("sinkd"), None, ALU.max))
            ch.step(V.tensor_scalar(st[:, 2:4], st[:, 0:2], -1.0, None, ALU.mult))
            V.tensor_scalar(st[:, 4:6], st[:, 2:4], pc("sinkd"), None, ALU.add).then_inc(s_dnm, 1)
            dve.wait_ge(s_de, 1)
            ch.step(V.tensor_tensor(st[:, 10:12], st[:, 6:8], st[:, 8:10], ALU.add))
            ch.step(V.reciprocal(st[:, 12:14], st[:, 10:12]))
            ch.step(V.tensor_scalar(pd[:, 0, :], pd[:, 0, :], st[:, 12:13], None, ALU.mult))
            V.tensor_scalar(pd[:, 1, :], pd[:, 1, :], st[:, 13:14], None, ALU.mult).then_inc(s_dp, 1)
            dve.wait_ge(s_lb, 1)
            ch.step(V.tensor_tensor(small[:, 24:28], small[:, 28:32], small[:, 32:36], ALU.add))
            ch.step(V.reciprocal(small[:, 24:28], small[:, 24:28]))
            ch.step(V.tensor_tensor(lb, small[:, 28:32], small[:, 24:28], ALU.mult))
            ch.step(V.tensor_scalar(oml, lb, -1.0, 1.0, ALU.mult, ALU.add))
            dve.wait_ge(s_ha, 2)
            for h in range(4):
                ch.done(V.tensor_scalar(hT1[:, h, :], hT1[:, h, :], oml[:, h:h + 1], lb[:, h:h + 1],
                                        ALU.mult, ALU.add))
                ch.done(V.tensor_scalar(hK[:, h, :], hK[:, h, :], oml[:, h:h + 1], None, ALU.mult))
            ch.sync()
            V.memset(small[:, 3:4], 0.0).then_inc(s_hd, 1)
            dve.wait_ge(s_ha, 3)
            dve.wait_ge(s_reset, 16)
            for h in range(4):
                ch.done(V.tensor_tensor_scan(gates[:, h, :], resm, hT1[:, h, :], 0.0, ALU.mult, ALU.add))
            ch.sync()

            def views(a, i=None):
                out = []
                for h in range(4):
                    for lo, hi_, C in ((0, NP, 16), (NP, NT, ST)):
                        v = a[:, h, lo:hi_].rearrange("p (c t) -> p c t", t=C)
                        if i is not None:
                            m = (C // 2 - 1) if i == "mid" else C - 1
                            v = v[:, :, m:m + 1].to_broadcast([P, (hi_ - lo) // C, C])
                        out.append(v)
                return out
            b = gates[:, 0:4, :]
            for o, i0, i1 in zip(views(hT1), views(b), views(b, "mid")):
                ch.done(V.tensor_tensor(o, i0, i1, ALU.subtract))
            ch.sync()
            V.tensor_scalar(hT1[:, :, :], hT1[:, :, :], -80.0, 80.0, ALU.max, ALU.min).then_inc(s_hd, 1)
            dve.wait_ge(s_ha, 4)
            V.tensor_tensor(hQ1[:, :, :], gates[:, 4:8, :], hT2[:, :, :], ALU.mult).then_inc(s_hd, 1)
            dve.wait_ge(s_ha, 5)
            V.tensor_tensor(hK1[:, :, :], hK[:, :, :], hT2[:, :, :], ALU.mult).then_inc(s_hd, 1)
            for o, i0, i1 in zip(views(hT1), views(b, "last"), views(b)):
                ch.done(V.tensor_tensor(o, i0, i1, ALU.subtract))
            dve.wait_ge(s_hd, 3)
            dve.wait_ge(s_ha, 6)
            ch.sync()
            V.tensor_tensor(gates[:, 4:8, :], gates[:, 4:8, :], hT2[:, :, :], ALU.mult).then_inc(s_hd, 1)
            dve.wait_ge(s_hd, 5)
            dve.wait_ge(s_ha, 7)
            ch.step(V.tensor_tensor(hK[:, :, :], hK[:, :, :], hT2[:, :, :], ALU.mult))
            dve.wait_ge(s_ha, 8)
            dve.wait_ge(s_t, 16)
            ch.step(V.memset(am[:, :, :, :], 0.0))
            V.memset(S, 0.0).then_inc(s_S, 1)
            V.memset(small[:, 4:5], 0.0).then_inc(s_h, 1)
            tri = mcc("tri")[0:16, :].rearrange("p (h t) -> p h t", h=4).bitcast(U32)
            for s in range(NCH + 1):
                if s < NCH:
                    off, C = CHUNKS[s]
                    dve.wait_ge(s_at, s + 1)
                    if s >= 2:
                        dve.wait_ge(s_oc, s - 1)
                    V.copy_predicated(am[0:C, s % 2, :, 0:C], tri[0:C, :, 0:C],
                                      PB[0][0:C, 0, 0:64].rearrange("p (h t) -> p h t", h=4)[:, :, 0:C])\
                        .then_inc(s_am, 1)
                if s >= 1:
                    q = s - 1
                    bq = q - NPC
                    dve.wait_ge(s_kv, q + 1)
                    dst = S if bq < 0 else Ssm[bq % 2]
                    for h in range(4):
                        m = V.scalar_tensor_tensor(out=dst[:, h, :], in0=dst[:, h, :], scalar=hD[:, h, q:q + 1],
                                                   in1=PB[1][:, q % 2, h * P:(h + 1) * P],
                                                   op0=ALU.mult, op1=ALU.add)
                    m.then_inc(s_S, 1)
            for h in range(4):
                dve.wait_ge(s_hr, h + 1)
                ch.step(V.reciprocal(hT2[:, h, :], hT2[:, h, :]))
                ch.step(V.scalar_tensor_tensor(out=hO[:, h, :], in0=hO[:, h, :], scalar=pc("og"), in1=hT2[:, h, :],
                                               op0=ALU.mult, op1=ALU.mult))
                V.tensor_tensor(hO[:, h, :], hO[:, h, :], gates[:, 8 + h, :], ALU.mult).then_inc(s_mixf, 1)
            lo_parts([zq[:, h, :] for h in range(4)], "mix")
            lo_parts([hO[:, h, :] for h in range(4)], "mix", 4)

            def residual(t0, base):
                for i in range(KC):
                    dve.wait_ge(s_used, t0 + i + 1)
                    V.tensor_tensor(tok2(xt[:, i, :]), tok2(xt[:, i, :]), both(PA[(t0 + i) % 2]), ALU.add)\
                        .then_inc(s_res, 1)
            residual(T_OUT, 0)
            retrieval(0)
            experts(0)
            norm(2)
            ch.done(V.memset(up[:, :, 0:CW - 1], 0.0))
            dve.wait_ge(s_conv, 16 * KC)
            for m in range(KC):
                dve.wait_ge(s_used, T_PW1 + 2 * m + 1)
                dve.wait_ge(s_sg, m + 1)
                pa = PA[T_PW1 % 2]
                for o, i0, i1 in ((up[:, m, CW - 1:CW - 1 + HALF], pa[:, 0, 0:HALF], sg[:, m % 2, 0:HALF]),
                                  (up[:, m, CW - 1 + HALF:CW - 1 + NP], pa[:, 1, 0:NP - HALF],
                                   sg[:, m % 2, HALF:NP]),
                                  (us[:, m, :, CW - 1:CW - 1 + ST],
                                   pa[:, 1, NP - HALF:HALF].rearrange("p (b t) -> p b t", b=SB),
                                   sg[:, m % 2, NP:NT].rearrange("p (b t) -> p b t", b=SB))):
                    V.scalar_tensor_tensor(out=o, in0=i0, scalar=pc("b1", m), in1=i1,
                                           op0=ALU.add, op1=ALU.mult).then_inc(s_u, 1)
                dve.wait_ge(s_u, 3 * (m + 1))
                ch.sync()
                for i in range(CW):
                    w = pc("wdw", CW * m + i)
                    a0, a1 = up[:, m, i:i + NP], us[:, m, :, i:i + ST]
                    c0, c1 = cv[:, m, 0:NP], cv[:, m, NP:NT].rearrange("p (b t) -> p b t", b=SB)
                    if i == 0:
                        ch.done(V.tensor_scalar(c0, a0, w, pc("bdw", m), ALU.mult, ALU.add))
                        ch.done(V.tensor_scalar(c1, a1, w, pc("bdw", m), ALU.mult, ALU.add))
                        ch.sync()
                    else:
                        ch.done(V.scalar_tensor_tensor(out=c0, in0=a0, scalar=w, in1=c0,
                                                       op0=ALU.mult, op1=ALU.add))
                        x1 = V.scalar_tensor_tensor(out=c1, in0=a1, scalar=w, in1=c1,
                                                    op0=ALU.mult, op1=ALU.add)
                        if i < CW - 1:
                            ch.done(x1)
                        ch.sync()
                x1.then_inc(s_cv, 1)
            dve.wait_ge(s_ms, 1)
            ch.step(V.tensor_scalar(tok2(sg[:, 0, :]), both(PB[0]), 1.0 / D, None, ALU.mult))
            for k in range(KC):
                V.tensor_tensor(cv[:, k, :], cv[:, k, :], sg[:, 0, :], ALU.subtract).then_inc(s_cen, 1)
            dve.wait_ge(s_cr, 1)
            ch.step(V.reciprocal(root[:, :], root[:, :]))
            for k in range(KC):
                V.scalar_tensor_tensor(out=cv[:, k, :], in0=cv[:, k, :], scalar=pc("lng", k), in1=root[:, :],
                                       op0=ALU.mult, op1=ALU.mult).then_inc(s_ln, 1)
            for k in range(KC):
                dve.wait_ge(s_si, k + 1)
            lo_parts([cv[:, k, :] for k in range(KC)], "ln")
            residual(T_PW2, 8)
            retrieval(1)
            experts(1)

        @block.gpsimd
        def _(pool):
            def lo(t, slot, buf):
                pool.wait_ge(s_hi, t + 1)
                nc.gpsimd.tensor_tensor(ring_lo[:, slot, :], raw[buf][:], ring_hi[:, slot, :].bitcast(F32),
                                        ALU.subtract).then_inc(s_lo, 1)

            def lo_run(a, b):
                n = (b - a) // SLOTS
                if n >= 2:
                    with pool.Fori(0, n) as i:
                        for u in range(SLOTS):
                            lo(8 * i + (a + u), (a + u) % SLOTS, (a + u) % 2)
                    a += n * SLOTS
                for t in range(a, b):
                    lo(t, t % SLOTS, t % 2)

            lo_run(0, N_IN)
            pool.wait_ge(s_used, N_IN)
            pool.dma_start(kcat[:, :, 0:WIN], kcacheT).then_inc(s_dload, 16)
            pool.dma_start(vcat[:, :, :], vcache).then_inc(s_dload, 16)
            pool.wait_ge(s_qr, 5)
            pool.dma_start(resm, reset).then_inc(s_reset, 16)
            pool.wait_ge(s_o, 16)
            for b in range(SB):
                if b >= 2:
                    pool.wait_ge(s_so[b % 2], 16 * (b // 2))
                pool.dma_start(Ssm[b % 2], state_h[b].rearrange("h k v -> k h v")).then_inc(s_sl[b % 2], 16)
                if b >= 1:
                    pool.wait_ge(s_S, 1 + NPC + b)
                    pool.dma_start(hs_s[b - 1].rearrange("h k v -> k h v"), Ssm[(b - 1) % 2])\
                        .then_inc(s_so[(b - 1) % 2], 16)
            pool.wait_ge(s_S, 1 + NCH)
            pool.dma_start(hs_s[SB - 1].rearrange("h k v -> k h v"), Ssm[(SB - 1) % 2]).then_inc(s_so[(SB - 1) % 2], 16)
            pool.dma_start(hs_p.rearrange("h k v -> k h v"), S).then_inc(s_so[0], 16)
            pool.wait_ge(s_so[0], 16 * (SB // 2 + 1))
            pool.wait_ge(s_so[1], 16 * (SB // 2))
            lo_run(T_OUT, T_OUT + N_OUT)
            pool.wait_ge(s_res, 1)
            pool.dma_start(keys[:, :, :], keysT[0]).then_inc(s_keys, 16)
            lo_run(T_WQ[0], T_WQ[0] + N_WQ)
            lo_run(T_EXP[0], T_EXP[0] + N_EXP)
            pool.wait_ge(s_wl, NKEY)
            pool.wait_ge(s_used, T_EXP[0] + N_EXP)
            for k in range(KC):
                pool.dma_start(us[:, k, :, 0:CW - 1], convT[k * P:(k + 1) * P]).then_inc(s_conv, 16)
            lo_run(T_PW1, T_PW2 + KC)
            pool.wait_ge(s_res, 9)
            pool.wait_ge(s_out, 16 * 15)
            pool.dma_start(keys[:, :, :], keysT[1]).then_inc(s_keys, 16)
            lo_run(T_WQ[1], T_WQ[1] + N_WQ)
            lo_run(T_EXP[1], T_EXP[1] + N_EXP)


_OUTS = [("yT", (D, NT)), ("kwin_p", (P, P)), ("vwin_p", (P, P)), ("s_p", (4, P, P)), ("cb_p", (D, CW - 1)),
         ("kwin_s", (SB, WIN, P)), ("vwin_s", (SB, WIN, P)), ("s_s", (SB, 4, P, P)), ("cb_s", (D, SB, CW - 1))]


def kernel(**inputs):
    import numpy as np
    import concourse.bacc as _bacc
    from concourse import mybir as _mybir
    from concourse.bass_utils import run_bass_kernel_spmd as _run
    i = {k: np.asarray(v) for k, v in inputs.items()}
    f32 = np.float32

    def chan(v, w=1):
        return v.reshape(-1, P).T

    def tiles(w):
        return w.reshape(KC, P, -1, P).transpose(2, 1, 0, 3).reshape(-1, P, D)

    order = [h for j in range(4) for h in (j, 4 + j)]
    w_in = i["w_in0"]
    q = w_in[:, 0:512].reshape(D, 8, HD)[:, order].reshape(D, 512)
    k, v = w_in[:, 512:640], w_in[:, 640:768]
    qb, fb, ib, gb = (w_in[:, 768 + 512 * n:768 + 512 * (n + 1)] for n in range(4))
    w_out = i["w_out0"]
    wo = np.concatenate([w_out[0:512].reshape(8, HD, D)[order].reshape(512, D), w_out[512:]], 0)
    pw1 = i["conv_w_pw1"].reshape(D, 2, KC, P).transpose(0, 2, 1, 3).reshape(D, 2 * D)
    parts = [tiles(x) for x in (q, k, v, fb, qb, gb, ib, wo, i["peer_w_q"][0])]

    def expert_tiles(l):
        u = i["peer_u"][l].reshape(NKEY, P, KC, P).transpose(0, 3, 2, 1).reshape(NKEY, P, D)
        w = i["peer_v"][l].reshape(NKEY, P, D)
        out = [u[0:1]]
        for g in range(NG):
            out += [u[4 * g + 1:4 * g + 5], w[4 * g:4 * g + 4]]
        return out
    parts += expert_tiles(0)
    parts += [tiles(pw1), tiles(i["conv_w_pw2"]), tiles(i["peer_w_q"][1])]
    parts += expert_tiles(1)
    stream = np.concatenate(parts, 0)

    xT = np.concatenate([i["x_prompt"].reshape(NP, D), i["x_sample"].reshape(NS, D)], 0).T
    par = np.zeros((P, NPAR), f32)

    def put(n, a):
        par[:, PC[n][0]:PC[n][0] + PC[n][1]] = a
    for n, a in (("g_mix0", i["norm_mix_g"][0]), ("g_mix1", i["norm_mix_g"][1]), ("g_ffn0", i["norm_ffn_g"][0]),
                 ("g_ffn1", i["norm_ffn_g"][1]), ("lb0", i["hgrn_lb"][0]), ("lb1", i["hgrn_lb"][1]),
                 ("og", i["hgrn_o_norm_g"]), ("b1", i["conv_b_pw1"]), ("bdw", i["conv_b_dw"]),
                 ("lng", i["conv_ln_g"]), ("lnb", i["conv_ln_b"])):
        put(n, chan(a))
    put("gq", np.concatenate([i["attn_q_norm_g"]] * 2)[:, None])
    put("gk", np.concatenate([i["attn_k_norm_g"]] * 2)[:, None])
    put("sink", np.broadcast_to(i["attn_sinks"][order][None, :], (P, 8)))
    put("sinkd", np.broadcast_to(i["attn_sinks"].reshape(1, 8, 1), (4, 8, ST)).reshape(P, 1))
    put("wdw", i["conv_w_dw"].reshape(CW, KC, P).transpose(2, 1, 0).reshape(P, KC * CW))

    con = np.zeros((P, NCON), f32)
    con[:, 0:128] = np.eye(P)
    con[:, 128:256] = 1.0
    con[:, 256:384] = np.arange(P)[None, :]
    con[:, 384:399] = np.array(CAND_AT[1:])[None, :]
    con[:, 399:414] = np.diff(np.array(CAND_AT))[None, :]
    mcn = np.zeros((P, NMC), f32)
    r = np.arange(P)
    mcn[:, 0:128] = (r[:, None] // HD == r[None, :] // HD)
    rot = np.zeros((P, P), f32)
    for b in (0, HD):
        for a in range(8):
            rot[b + a + 8, b + a] = -1.0
            rot[b + a, b + a + 8] = 1.0
    mcn[:, 128:256] = rot
    qi, ki = np.arange(WIN)[:, None], np.arange(2 * WIN)[None, :]
    dist = qi + WIN - ki
    ok = (dist >= 0) & (dist < WIN)
    mcn[:, 256:512] = np.where(ok, 0.0, -1e30)
    mcn[:, 512:768] = np.where(ok & (ki >= WIN), 0.0, -1e30)
    dist = (WIN + r[:, None] % ST) - np.arange(WIN + ST)[None, :]
    mcn[:, 768:900] = np.where((dist >= 0) & (dist < WIN), 0.0, -1e30)
    tri = (np.arange(16)[:, None] <= np.arange(16)[None, :]).astype(f32)
    mcn[0:16, 900:964] = np.tile(tri, (1, 4))
    inv = (f32(500000.0) ** (-np.arange(0, 16, 2, dtype=f32) / f32(16))).astype(f32)
    posn = np.concatenate([np.arange(NP), np.tile(1024 + np.arange(ST), SB)]).astype(f32)
    ang = (posn[:, None] * inv[None, :]).astype(f32)
    cos, sin = np.ones((P, NT), f32), np.zeros((P, NT), f32)
    for b in (0, 8, HD, HD + 8):
        cos[b:b + 8], sin[b:b + 8] = np.cos(ang).T, np.sin(ang).T
    mcn[:, 964:964 + NT], mcn[:, 964 + NT:] = cos, sin
    reset = np.ones((P, NT), f32)
    for off, _ in CHUNKS:
        reset[:, off] = 0.0

    kc = i["cache_swa_k"].reshape(SB, WIN, P)
    vc = i["cache_swa_v"].reshape(SB, WIN, P)
    arrays = {
        "xT": xT, "stream": stream, "params": par, "consts": con, "mconsts": mcn, "reset": reset,
        "keysT": i["peer_keys"].reshape(2, 16, NKEY, P).transpose(0, 3, 1, 2),
        "kcacheT": kc.transpose(2, 0, 1), "vcache": vc.transpose(1, 0, 2), "kvcache_n": np.stack([kc, vc]),
        "state_h": i["state_hgrn"], "convT": i["state_conv"].transpose(2, 0, 1),
    }
    nc = _bacc.Bacc("TRN2", target_bir_lowering=False, num_devices=1)
    args, feed = [], {}
    for n, a in arrays.items():
        a = np.ascontiguousarray(a)
        feed[f"in_{n}"] = a
        args.append(nc.dram_tensor(f"in_{n}", a.shape, _mybir.dt.from_np(a.dtype), kind="ExternalInput").ap())
    for n, shape in _OUTS:
        args.append(nc.dram_tensor(f"out_{n}", shape, _mybir.dt.float32, kind="ExternalOutput").ap())
    build(nc, *args)
    o = _run(nc, [feed], core_ids=[0]).results[0]
    y = o["out_yT"].T
    return (y[:NP].reshape(1, NP, D), y[NP:].reshape(SB, ST, D),
            o["out_kwin_p"].reshape(1, WIN, 2, HD), o["out_vwin_p"].reshape(1, WIN, 2, HD),
            o["out_s_p"].reshape(1, 4, P, P), o["out_cb_p"].T.reshape(1, CW - 1, D),
            o["out_kwin_s"].reshape(SB, WIN, 2, HD), o["out_vwin_s"].reshape(SB, WIN, 2, HD),
            o["out_s_s"], o["out_cb_s"].transpose(1, 2, 0))
```

```python
from contextlib import ExitStack

import concourse.bass as bass
from concourse import mybir

F32 = mybir.dt.float32
F32R = mybir.dt.float32r
U32 = mybir.dt.uint32
ALU = mybir.AluOpType
ACT = mybir.ActivationFunctionType
X = mybir.AxisListType.X

P = 128
D = 1024
KC = D // P
NP, NS, SB, ST = 512, 32, 8, 4
NT = NP + NS
HALF = NT // 2
NTILE = 5
ROWS = [128, 128, 128, 128, 32]
EPS = 1e-6
HD, WIN = 64, 128
HPEER, TOPK, NKEY = 8, 16, 128
NBLK = NP // P
CW = 31
SCALE = HD ** -0.5
CONV_DVE, CONV_PE = ((0, 1), (2, 3), (4, 5)), (6, 7)
NDIAG = 33
N_SEL = 15
ACT_OH_IDLE, ACT_OH = 2, (4, 4, 5, 4, 4, 3, 6, 6, 6, 5, 6, 5, 4, 4, 3)

T_IN, N_IN = 0, 22
T_OUT, N_OUT = 22, 8
T_WQ = [30, 342 - 16]
N_WQ = 16
T_EXP = [46, 342]
N_EXP = 256
T_PW1, T_PW2 = 302, 318
N_TILES = 598
GRP = 4
NG = NKEY // GRP
LOOK = 4
SLOTS = 8

CAND_W = [TOPK // (a + 1) for a in range(TOPK)]
CAND_AT = [sum(CAND_W[:a]) for a in range(TOPK)]
NCAND = sum(CAND_W)

CHUNKS = [(16 * c, 16) for c in range(NP // 16)] + [(NP + ST * b, ST) for b in range(SB)]
NPC = NP // 16
NCH = len(CHUNKS)
HPART = [(0, NP), (NP, NT)]
CPT = 8

PC = {}
_at = 0
for _n, _w in (("g_mix0", 8), ("g_ffn0", 8), ("g_mix1", 8), ("g_ffn1", 8), ("gq", 1), ("gk", 1), ("sink", 8),
               ("sinkd", 1), ("lb0", 4), ("lb1", 4), ("og", 1), ("b1", 16), ("wdw", 8 * CW), ("bdw", 8),
               ("lng", 8), ("lnb", 8)):
    PC[_n] = (_at, _w)
    _at += _w
NPAR = _at
CC = {"ident": (0, 128), "ones": (128, 128), "iota": (256, 128), "start": (384, 15), "dstart": (399, 15)}
NCON = 414
MC = {"blk": (0, 128), "rot": (128, 128), "band": (256, 256), "band0": (512, 256), "dec": (768, 132),
      "tri": (900, 128), "tri_s": (1028, NS), "rows": (1060, 8), "rows_s": (1068, 8),
      "cos": (1076, NT), "sin": (1076 + NT, NT)}
NMC = 1076 + 2 * NT


def act_tokens(n, q):
    return ACT_OH[q - 1] if 1 <= q <= N_SEL and n + 1 < NTILE else ACT_OH_IDLE


def build(nc, xT, stream, params, consts, mconsts, reset, keysT, kcacheT, vcache, kvcache_n, state_h, convT,
          yT, kwin_p, vwin_p, hs_p, cb_p, kwin_s, vwin_s, hs_s, cb_s):
    ctx = ExitStack()
    with ctx:
        def sb(name, shape, dt=F32, where=ctx):
            return where.enter_context(nc.sbuf_tensor(name, shape, dt))

        def sem(name):
            return ctx.enter_context(nc.semaphore(name))

        xt = sb("xt", [P, KC, NT])
        hh = sb("hh", [P, KC, NT], F32R)
        hl = sb("hl", [P, KC, NT], F32R)
        raw = [sb(f"raw{i}", [P, D]) for i in range(2)]
        par = sb("par", [P, NPAR])
        con = sb("con", [P, NCON])
        small = sb("small", [P, 64])
        root = sb("root", [P, NT])
        eps = small[:, 0:1]

        def pc(n, i=0, w=1):
            return par[:, PC[n][0] + i:PC[n][0] + i + w]

        def cc(n):
            return con[:, CC[n][0]:CC[n][0] + CC[n][1]]
        ident, ones, iota = cc("ident"), cc("ones"), cc("iota")

        with ExitStack() as z:
            ring_hi = sb("ring_hi", [P, SLOTS, D], F32R, z)
            ring_lo = sb("ring_lo", [P, SLOTS, D], F32R, z)
        with ExitStack() as z:
            hK = sb("hK", [P, 4, NT], F32, z)
            hQ1 = sb("hQ1", [P, 4, NT], F32, z)
            hK1 = sb("hK1", [P, 4, NT], F32, z)
            hT1 = sb("hT1", [P, 4, NT], F32, z)
            hT2 = sb("hT2", [P, 4, NT], F32, z)
            hD = sb("hD", [P, 4, NCH], F32, z)
            with ExitStack() as zz:
                hO = sb("hO", [P, 4, NT], F32, zz)
            with ExitStack() as zz:
                kcat = sb("kcat", [P, SB, WIN + ST], F32, zz)
                vcat = sb("vcat", [P, SB, P], F32, zz)
                vnew = sb("vnew", [ST, SB, P], F32, zz)
                qbd = sb("qbd", [P, SB, 2, 4, ST], F32, zz)
                pd = sb("pd", [P, 2, WIN + ST], F32, zz)
                pdT = sb("pdT", [P, 2, P], F32, zz)
                pdN = sb("pdN", [ST, 2, P], F32, zz)
        with ExitStack() as z:
            stage = sb("stage", [P, NKEY, P], F32, z)
        zone = sb("zone", [P, SLOTS * 2 * D])

        with ExitStack() as z:
            gates = sb("gates", [P, 16, NT], F32, z)
            hf_mix = gates[:, 0:8, :]
            zq = sb("zq", [P, 5, NT], F32, z)
            krp = sb("krp", [P, P + NT], F32, z)
            krz = sb("krz", [P, 2, P + NT], F32, z)
            vT = sb("vT", [P, NT], F32, z)
            vtok = sb("vtok", [P, NBLK + 1, P], F32, z)
            kvo = sb("kvo", [P, 3, P], F32, z)
            mc = sb("mc", [P, NMC], F32, z)
            scr = sb("scr", [P, 4, NT], F32, z)
            scr1 = scr[:, :, :].rearrange("p a n -> p (a n)")
            st8 = sb("st8", [P, 2, 16], F32, z)
        t1 = hT1[:, :, :].rearrange("p h n -> p (h n)")
        t2 = hT2[:, :, :].rearrange("p h n -> p (h n)")
        km = [t1[:, 512 * i:512 * i + 512].rearrange("p (h f) -> p h f", h=4) for i in range(2)]
        vt = [t1[:, 1024 + 512 * i:1536 + 512 * i].rearrange("p (h f) -> p h f", h=4) for i in range(2)]
        am = [t2[:, 512 * i:512 * i + 512].rearrange("p (h t) -> p h t", h=4) for i in range(2)]
        sqz = [scr[:, 0, :], scr[:, 1, :]]
        rt, rt2 = scr[:, 2, :], scr[:, 3, :]
        sm = [scr1[:, 512 * i:512 * i + 512].rearrange("p (g k) -> p g k", g=2) for i in range(2)]
        pT = [scr1[:, 1024 + 512 * i:1536 + 512 * i].rearrange("p (a q) -> p a q", a=4) for i in range(2)]
        Sb = [scr1[:, o:o + 512].rearrange("p (h v) -> p h v", h=4) for o in (0, 1536)]
        krz1 = krz[:, :, :].rearrange("p g n -> p (g n)")
        Ssm = [a[:, o:o + 512].rearrange("p (h v) -> p h v", h=4)
               for a, o in ((scr1, 512), (scr1, 1024), (krz1, 0), (krz1, 512))]

        def mcc(n):
            return mc[:, MC[n][0]:MC[n][0] + MC[n][1]]
        resm = mcc("cos")
        with ExitStack() as z:
            with ExitStack() as zz:
                hf_peer = sb("hf_peer", [P, KC, NT], F32, zz)
            with ExitStack() as zz:
                oh2 = sb("oh2", [P, 2, 8, P], F32, zz)
                oh1 = sb("oh1", [P, 2, 8, P], F32, zz)
            sb("ohpad", [P, KC * NT], F32, z)
            with ExitStack() as zz:
                keys = sb("keys", [P, 16, P], F32, zz)
                qh = sb("qh", [P, 2, NT], F32, zz)
                sc2 = sb("sc2", [P, NTILE, P], F32, zz)
            with ExitStack() as zz:
                ge = [sb(f"ge{f}", [P, 4, 16, 16], F32, zz) for f in range(2)]
                tm_a = sb("tm_a", [P, 4, 16, 16], F32, zz)
            sb("keypad", [P, 16 * P + 2 * NT + NTILE * P], F32, z)
            with ExitStack() as zz:
                sb("experts_above", [P, 576], F32, zz)
                stage_s = sb("stage_s", [P, NKEY, NS], F32, zz)
            sv = sb("sv", [P, NTILE, 16, 16], F32, z)
            si = sb("si", [P, NTILE, 16, 16], U32, z)
            sif = sb("sif", [P, 16, 16], F32, z)
            cand = sb("cand", [P, 8, NCAND], F32, z)
            cand2 = sb("cand2", [P, 8, NCAND], F32, z)
            fv = sb("fv", [P, 8, 16], F32, z)
            fi = sb("fi", [P, 8, 16], U32, z)
            pos = sb("pos", [P, 8, 16], F32, z)
            dsi = sb("dsi", [P, 8, 15], F32, z)
            tm = [tm_a, sb("tm_b", [P, 4, 16, 16], F32, z)]
            tm2 = [sb(f"tm2_{f}", [P, 4, 16, 16], F32, z) for f in range(2)]
            sel = sb("sel", [P, 3, 8, 16], F32, z)
            r16 = sb("r16", [P, 8, 16], F32, z)
            r8 = sb("r8", [P, 2, 8], F32, z)
            slT = sb("slT", [P, 3, NT], F32, z)
            dist = sb("dist", [P, 2, max(ACT_OH), P], F32, z)
        with ExitStack() as z:
            wh = sb("wh", [P, 5, NT], F32R, z)
            wl = sb("wl", [P, 5, NT], F32R, z)
            gt = sb("gt", [P, GRP, NT], F32, z)
            ga = sb("ga", [P, 2, NT], F32, z)
        with ExitStack() as z:
            up = sb("up", [P, KC, CW - 1 + NP], F32, z)
            us = sb("us", [P, KC, SB, CW - 1 + ST], F32, z)
            cv = sb("cv", [P, KC, NT], F32, z)
            with ExitStack() as zz:
                diag = sb("diag", [P, NDIAG, P], F32, zz)
            hf_conv = sb("hf_conv", [P, KC, NT], F32, z)
            sg = sb("sg", [P, 2, NT], F32, z)
        sb("arena", [P, 19800])

        psum = [ctx.enter_context(nc.psum_tensor(f"bank{i}", [P, 2, 512], F32)) for i in range(4)]
        PA, PB = psum[0:2], psum[2:4]
        PCV = PB

        def tok2(ap):
            return ap.rearrange("p (a n) -> p a n", a=2)

        def both(pair):
            return pair[:, :, 0:HALF]

        gdram = nc.dram_tensor("gate_matrix", [2, NKEY, P, NT], F32, kind="Internal").ap()

        s_par = sem("params_loaded")
        s_x = sem("x_loaded")
        s_mc = sem("mixer_consts_loaded")
        s_keys = sem("keys_loaded")
        s_dload = sem("decode_cache_loaded")
        s_reset = sem("reset_mask_loaded")
        s_conv = sem("conv_state_loaded")
        s_raw = [sem(f"raw{i}_loaded") for i in range(2)]
        s_hi = sem("hi_ready")
        s_lo = sem("lo_ready")
        s_used = sem("tile_used")
        s_eps = sem("small_consts_ready")
        s_sq = sem("squares_ready")
        s_sum = sem("norm_sum_done")
        s_root = sem("norm_root_ready")
        s_hf = sem("normed_ready")
        s_hh = sem("normed_hi_ready")
        s_hl = sem("normed_lo_ready")
        s_ev = sem("projection_evacuated")
        s_res = sem("residual_added")
        s_v = sem("dve_chain")
        s_a = sem("act_chain")
        s_out = sem("outputs_written")

        V = nc.vector
        A = nc.scalar
        T = nc.tensor

        class Chain:
            def __init__(self, eng, s):
                self.eng, self.s, self.n = eng, s, 0

            def done(self, ins):
                self.n += 1
                ins.then_inc(self.s, 1)

            def sync(self):
                self.eng.wait_ge(self.s, self.n)

            def step(self, ins):
                self.done(ins)
                self.sync()

        block = ctx.enter_context(nc.Block())

        @block.sync
        def _(sp):
            sp.dma_start(xt[:], xT.rearrange("(k p) n -> p k n", p=P)).then_inc(s_x, 16)
            for t in range(2):
                sp.dma_start(raw[t][:], stream[t]).then_inc(s_raw[t], 16)
            with sp.Fori(1, N_TILES // 2) as i:
                for u in range(2):
                    sp.wait_ge(s_lo, 2 * i + u - 1)
                    sp.dma_start(raw[u][:], stream[bass.ds(2 * i + u, 1)].rearrange("a p n -> (a p) n"))\
                      .then_inc(s_raw[u], 16)

        s_qsum = sem("qk_sum_done")
        s_qroot = sem("qk_root_ready")
        s_qn = sem("qk_normed")
        s_qrot = sem("qk_rotated")
        s_qr = sem("qk_roped")
        s_vt = sem("v_transposed")
        s_vev = sem("v_tokens_ready")
        s_pad = sem("pads_zeroed")
        s_s = sem("scores_done")
        s_sm = sem("masked_scores_ready")
        s_nm = sem("neg_max_ready")
        s_pe = sem("exps_ready")
        s_p = sem("probs_ready")
        s_t = sem("probs_transposed")
        s_pt = sem("probs_T_ready")
        s_o = sem("attn_done")
        s_oe = sem("attn_evacuated")
        s_dq = sem("decode_q_ready")
        s_dv = sem("decode_v_ready")
        s_ds = sem("decode_scores_done")
        s_dnm = sem("decode_neg_max_ready")
        s_de = sem("decode_exps_ready")
        s_dp = sem("decode_probs_ready")
        s_dt = sem("decode_probs_transposed")
        s_dpt = sem("decode_probs_T_ready")
        s_do = sem("decode_attn_done")
        s_dend = sem("decode_attn_stored")
        s_h = sem("hgrn_operands_ready")
        s_hd = sem("hgrn_dve_stage")
        s_lbx = sem("lower_bound_shifted")
        s_lb = sem("lower_bound_exps_ready")
        s_ha = sem("hgrn_act_stage")
        s_tr = sem("tile_k_v_transposed")
        s_vtile = sem("tile_v_ready")
        s_km = sem("chunk_k_ready")
        s_at = sem("tile_scores_done")
        s_am = sem("tile_scores_masked")
        s_oc = sem("chunk_out_done")
        s_oce = sem("tile_out_evacuated")
        s_kv = sem("chunk_kv_done")
        s_S = sem("state_updated")
        s_sl = [sem(f"sample_state_loaded{i}") for i in range(4)]
        s_so = [sem(f"sample_state_stored{i}") for i in range(4)]
        s_hsp = sem("prompt_state_stored")
        s_hsq = sem("head_squares_ready")
        s_hs = sem("head_sum_done")
        s_hr = sem("head_root_ready")
        s_mixf = sem("mixer_out_ready")
        s_sc = sem("key_scores_done")
        s_scf = sem("key_scores_read")
        s_gx = sem("gate_shifted")
        s_ge = sem("gate_exp_ready")
        s_sel = sem("selection_ready")
        s_selT = sem("selection_transposed")
        s_slT = sem("selection_T_ready")
        s_oh = sem("dve_onehots_ready")
        s_oha = sem("act_onehots_ready")
        s_eq = sem("key1_onehots_ready")
        s_ohp = sem("weighted_onehots_ready")
        s_gm = sem("gate_tokens_done")
        s_gs = sem("gate_tokens_staged")
        s_gw = [sem(f"gate_matrix_written{i}") for i in range(2)]
        s_cmp = sem("select_comparisons_ready")
        s_prd = sem("select_products_ready")
        s_gld = [sem(f"gate_tile{i}_loaded") for i in range(GRP)]
        s_ga = sem("gelu_ready")
        s_w = sem("gated_ready")
        s_wh = sem("gated_hi_ready")
        s_wl = sem("gated_lo_ready")
        s_y = sem("expert_out_done")
        s_ya = sem("expert_out_added")
        s_sg = sem("glu_sigmoid_ready")
        s_u = sem("glu_ready")
        s_dg = sem("tap_diagonal_ready")
        s_dgu = sem("tap_diagonal_used")
        s_cvp = [sem(f"conv_done{k}") for k in range(KC)]
        s_ms = sem("mean_sum_done")
        s_cen = sem("centered")
        s_csq = sem("centered_squares_ready")
        s_vs = sem("var_sum_done")
        s_cr = sem("ln_root_ready")
        s_ln = sem("ln_ready")
        s_si = sem("ln_silu_ready")

        def wait_x(eng, n, k):
            if n == 0:
                if k == 0:
                    eng.wait_ge(s_x, 16)
            elif n == 1:
                eng.wait_ge(s_res, k + 1)
            elif n == 2:
                eng.wait_ge(s_ya, 8 * (NG - 1) + k + 1)
            else:
                eng.wait_ge(s_res, 8 + k + 1)
        SUMS = [PA[0], PB[0], PA[0], PB[0]]
        HF = [hf_mix, hf_peer, hf_conv, hf_peer]
        GN = ["g_mix0", "g_ffn0", "g_mix1", "g_ffn1"]

        H_EVENT = {"n0": 0, "mix": 1, "n1": 2, "n2": 3, "ln": 4, "n3": 5}

        @block.tensor
        def _(pe):
            def norm(n):
                hf = HF[n]
                if n == 2:
                    pe.wait_ge(s_ga, NKEY)
                for k in range(KC):
                    pe.wait_ge(s_sq, 8 * n + k + 1)
                    for a in range(2):
                        m = T.matmul(SUMS[n][:, a, 0:HALF], ones, hf[:, k, a * HALF:(a + 1) * HALF],
                                     start=(k == 0), stop=(k == KC - 1))
                m.then_inc(s_sum, 1)

            def proj(t, first=False, event=None):
                pe.wait_ge(s_lo, t + 1)
                for k in range(KC):
                    if first:
                        pe.wait_ge(s_hl, 8 * H_EVENT[event] + k + 1)
                    for i, (w, h) in enumerate(((ring_hi, hh), (ring_hi, hl), (ring_lo, hh))):
                        for a in range(2):
                            m = T.matmul(PA[t % 2][:, a, 0:HALF], w[:, t % SLOTS, k * P:(k + 1) * P],
                                         h[:, k, a * HALF:(a + 1) * HALF],
                                         start=(k == 0 and i == 0), stop=(k == KC - 1 and i == 2))
                m.then_inc(s_used, 1)

            def qk_sum(j):
                pe.wait_ge(s_ev, j + 1)
                if j >= 1:
                    pe.wait_ge(s_qroot, j)
                for a in range(2):
                    m = T.matmul(PB[0][:, a, 0:HALF], mcc("blk"), sqz[j % 2][:, a * HALF:(a + 1) * HALF],
                                 start=True, stop=True)
                m.then_inc(s_qsum, 1)

            def qk_rot(j):
                pe.wait_ge(s_qn, j + 1)
                if j >= 1:
                    pe.wait_ge(s_qr, j)
                for a in range(2):
                    m = T.matmul(PB[1][:, a, 0:HALF], mcc("rot"), zq[:, j, a * HALF:(a + 1) * HALF],
                                 start=True, stop=True)
                m.then_inc(s_qrot, 1)

            def kv_tokens():
                pe.wait_ge(s_qr, 5)
                pe.wait_ge(s_ev, 6)
                for b in range(NBLK):
                    T.transpose(PB[0][:, 0, b * P:(b + 1) * P], vT[:, b * P:(b + 1) * P], ident)
                T.transpose(PB[0][:, 1, 0:P], krp[:, NP:NP + P], ident)
                T.transpose(PB[0][0:NS, 1, P:2 * P], krp[:, P + NP:P + NT], ident)
                T.transpose(PB[0][0:NS, 1, 2 * P:3 * P], vT[:, NP:NT], ident).then_inc(s_vt, 1)

            def scores(u):
                blk, j = divmod(u, 4)
                if u >= 2:
                    pe.wait_ge(s_sm, u - 1)
                else:
                    pe.wait_ge(s_vev, 2)
                    pe.wait_ge(s_pad, 4)
                for g in range(2):
                    m = T.matmul(PB[0][:, u % 2, g * 256:(g + 1) * 256], zq[:, j, blk * P:(blk + 1) * P],
                                 krz[:, g, blk * P:blk * P + 256], start=True, stop=True)
                m.then_inc(s_s, 1)

            def p_transpose(u):
                pe.wait_ge(s_p, u + 1)
                if u >= 1:
                    pe.wait_ge(s_pt, u)
                for g in range(2):
                    for b in range(2):
                        m = T.transpose(PB[1][:, 0, (2 * g + b) * P:(2 * g + b + 1) * P],
                                        sm[u % 2][:, g, b * P:(b + 1) * P], ident)
                m.then_inc(s_t, 1)

            def pv(u):
                blk, j = divmod(u, 4)
                pe.wait_ge(s_pt, u + 1)
                if u >= 1:
                    pe.wait_ge(s_oe, u)
                for g in range(2):
                    for b in range(2):
                        m = T.matmul(PB[1][64 * g:64 * g + 64, 1, 0:P],
                                     vtok[:, blk + b, 64 * g:64 * g + 64], pT[u % 2][:, 2 * g + b, :],
                                     start=(b == 0), stop=(b == 1))
                m.then_inc(s_o, 1)

            def decode():
                pe.wait_ge(s_dq, 1)
                pe.wait_ge(s_oe, 16)
                for b in range(SB):
                    T.transpose(PA[0][0:ST, b // 4, (b % 4) * P:(b % 4 + 1) * P],
                                vT[:, NP + ST * b:NP + ST * b + ST], ident)
                for b in range(SB):
                    m = T.matmul(PB[0][32 * (b % 4):32 * (b % 4) + 32, b // 4, 0:WIN + ST],
                                 qbd[:, b, :, :, :].rearrange("p g r t -> p (g r t)"), kcat[:, b, :],
                                 start=True, stop=True)
                m.then_inc(s_ds, 1)
                pe.wait_ge(s_dp, 1)
                for c in range(2):
                    T.transpose(PB[1][:, 0, c * P:(c + 1) * P], pd[:, c, 0:WIN], ident)
                for c in range(2):
                    m = T.transpose(PB[1][0:ST, 0, (2 + c) * P:(3 + c) * P], pd[:, c, WIN:WIN + ST], ident)
                m.then_inc(s_dt, 1)
                pe.wait_ge(s_dpt, 1)
                for b in range(SB):
                    q = slice(32 * (b % 4), 32 * (b % 4) + 32)
                    T.matmul(PB[1][:, 1, 32 * b:32 * b + 32], vcat[:, b, :], pdT[:, b // 4, q],
                             start=True, stop=False)
                    m = T.matmul(PB[1][:, 1, 32 * b:32 * b + 32], vnew[:, b, :], pdN[:, b // 4, q],
                                 start=False, stop=True)
                m.then_inc(s_do, 1)

            def tile_scores(b):
                off, R = b * P, ROWS[b]
                if b >= 2:
                    pe.wait_ge(s_km, CPT * (b - 1))
                    pe.wait_ge(s_vtile, b - 1)
                for h in range(4):
                    T.transpose(PA[b % 2][0:R, 0, h * P:(h + 1) * P], hK[:, h, off:off + R], ident)
                for h in range(4):
                    m = T.transpose(PA[b % 2][0:R, 1, h * P:(h + 1) * P], gates[:, 12 + h, off:off + R], ident)
                m.then_inc(s_tr, 1)
                if b >= 2:
                    pe.wait_ge(s_oce, b - 1)
                for h in range(4):
                    m = T.matmul(PB[0][0:R, b % 2, h * P:h * P + R], hK1[:, h, off:off + R],
                                 hQ1[:, h, off:off + R], start=True, stop=True)
                m.then_inc(s_at, 1)

            def tile_out(b):
                R = ROWS[b]
                pe.wait_ge(s_am, b + 1)
                pe.wait_ge(s_vtile, b + 1)
                for h in range(4):
                    T.matmul(PB[0][:, b % 2, h * P:h * P + R], vt[b % 2][0:R, h, :], am[b % 2][0:R, h, 0:R],
                             start=(h == 0), stop=False)

            def chunk_kv(s):
                b = s // CPT
                R = ROWS[b]
                pe.wait_ge(s_km, s + 1)
                if s % CPT == 0:
                    pe.wait_ge(s_vtile, b + 1)
                if s >= 2:
                    pe.wait_ge(s_S, s)
                for h in range(4):
                    m = T.matmul(PB[1][:, s % 2, h * P:(h + 1) * P], km[s % 2][0:R, h, :],
                                 vt[b % 2][0:R, h, :], start=True, stop=True)
                m.then_inc(s_kv, 1)

            def chunk_out(s):
                off, C = CHUNKS[s]
                tb = s // CPT
                b = s - NPC
                st = Sb[s % 2] if b < 0 else Ssm[b % 4]
                if b >= 0:
                    pe.wait_ge(s_sl[b % 4], 16 * (b // 4 + 1))
                else:
                    pe.wait_ge(s_S, s + 1)
                for h in range(4):
                    c = h * P + off - tb * P
                    m = T.matmul(PB[0][:, tb % 2, c:c + C], st[:, h, :], gates[:, 4 + h, off:off + C],
                                 start=False, stop=(s % CPT == CPT - 1 and h == 3))
                m.then_inc(s_oc, 1)

            def head_sum(i, h):
                a, b = HPART[i]
                e = 4 * i + h
                pe.wait_ge(s_hsq, e + 1)
                if e >= 2:
                    pe.wait_ge(s_hr, e - 1)
                T.matmul(PA[1][:, h % 2, 0:b - a], ones, hK[:, h, a:b], start=True, stop=True)\
                    .then_inc(s_hs, 1)

            def retrieval(l):
                pe.wait_ge(s_keys, 16 * (l + 1))
                ev0 = N_IN + N_WQ * l
                for i in range(N_WQ + 1):
                    if i < N_WQ:
                        if i >= 2:
                            pe.wait_ge(s_ev, ev0 + i - 1)
                        proj(T_WQ[l] + i, i == 0, "n1" if l == 0 else "n3")
                    if i >= 1:
                        q = i - 1
                        pe.wait_ge(s_ev, ev0 + q + 1)
                        if q >= 2:
                            pe.wait_ge(s_scf, N_WQ * l + q - 1)
                        for n in range(NTILE):
                            m = T.matmul(PB[q % 2][0:ROWS[n], n // 4, (n % 4) * P:(n % 4 + 1) * P],
                                         qh[:, q % 2, n * P:n * P + ROWS[n]], keys[:, q, :],
                                         start=True, stop=True)
                        m.then_inc(s_sc, 1)

            def gate_matrix(l):
                for n in range(NTILE):
                    pe.wait_ge(s_sel, NTILE * l + n + 1)
                    if n == 0:
                        pe.wait_ge(s_scf, N_WQ * (l + 1))
                    else:
                        pe.wait_ge(s_slT, NTILE * l + n)
                    for i in range(3):
                        m = T.transpose(PB[0][:, 0, i * P:i * P + ROWS[n]],
                                        sel[0:ROWS[n], i, :, :].rearrange("p h r -> p (h r)"),
                                        ident[0:ROWS[n], 0:ROWS[n]])
                    m.then_inc(s_selT, 1)
                    for q in range(ROWS[n] // 8):
                        e = (NT // 8) * l + n * 16 + q
                        pe.wait_ge(s_oh, e + 1)
                        pe.wait_ge(s_oha, e + 1)
                        pe.wait_ge(s_ohp, e + 1)
                        if e - (NT // 8) * l >= 2:
                            pe.wait_ge(s_gs, e - 1)
                        for i in range(8):
                            m = T.matmul(PA[e % 2][:, i // 4, (i % 4) * P:(i % 4 + 1) * P],
                                         oh2[:, e % 2, i, :], oh1[:, e % 2, i, :], start=True, stop=True)
                        m.then_inc(s_gm, 1)

            def experts(l):
                t0 = T_EXP[l]
                base_e, base_y = NKEY * l, 8 * NG * l

                def act_in(slot, pair, t, e_free):
                    pe.wait_ge(s_lo, t)
                    pe.wait_ge(s_ga, e_free)
                    for k in range(KC):
                        for i, (w, h) in enumerate(((ring_hi, hh), (ring_hi, hl), (ring_lo, hh))):
                            for a in range(2):
                                m = T.matmul(PA[pair][:, a, 0:HALF], w[:, slot, k * P:(k + 1) * P],
                                             h[:, k, a * HALF:(a + 1) * HALF],
                                             start=(k == 0 and i == 0), stop=(k == KC - 1 and i == 2))
                    m.then_inc(s_used, 1)

                def act_out(slots, par_, g, t):
                    for c in range(KC):
                        if c == 0:
                            pe.wait_ge(s_lo, t)
                            pe.wait_ge(s_ya, base_y + 8 * g)
                        if c >= 2:
                            pe.wait_ge(s_ya, base_y + 8 * g + c - 1)
                        for j in range(GRP):
                            if c == 0:
                                pe.wait_ge(s_wl, base_e + 4 * g + j + 1)
                            ws = j if (j or not par_) else 4
                            for i, (w, h) in enumerate(((ring_hi, wh), (ring_hi, wl), (ring_lo, wh))):
                                for a in range(2):
                                    m = T.matmul(PB[c % 2][:, a, 0:HALF], w[:, slots[j], c * P:(c + 1) * P],
                                                 h[:, ws, a * HALF:(a + 1) * HALF],
                                                 start=(j == 0 and i == 0), stop=(j == GRP - 1 and i == 2))
                                    if c == KC - 1 and i == 2 and a == 1 and j < GRP - 1:
                                        m.then_inc(s_used, 1)
                        if c < KC - 1:
                            m.then_inc(s_y, 1)
                        else:
                            m.then_inc(s_used, 1)

                def group(g, par_, last=False):
                    t = t0 + 1 + 8 * g
                    n_u = 3 if last else 4
                    for j in range(1, n_u + 1):
                        act_in((t0 + j) % SLOTS, j % 2, t + j, base_e + 4 * g + j - 1)
                    sl = [(t0 + 1 + n_u + j) % SLOTS for j in range(GRP)]
                    act_out(sl, par_, g, t + n_u + GRP)

                pe.wait_ge(s_gs, (NT // 8) * (l + 1))
                pe.wait_ge(s_hl, 8)
                act_in(t0 % SLOTS, 0, t0 + 1, base_e)
                with pe.Fori(0, NG // 2 - 1) as i:
                    group(2 * i, 0)
                    group(2 * i + 1, 1)
                group(NG - 2, 0)
                group(NG - 1, 1, True)

            norm(0)
            for m in range(N_IN):
                if m >= 2:
                    pe.wait_ge(s_ev, m - 1)
                proj(T_IN + m, m == 0, "n0")
                if m == 0:
                    pe.wait_ge(s_mc, 16)
                if 1 <= m <= 5:
                    qk_sum(m - 1)
                if 2 <= m <= 6:
                    qk_rot(m - 2)
                if m == 7:
                    kv_tokens()
                if m >= 8:
                    for u in (2 * (m - 8), 2 * (m - 8) + 1):
                        if u < 16:
                            scores(u)
                        if 0 <= u - 2 < 16:
                            p_transpose(u - 2)
                        if 0 <= u - 3 < 16:
                            pv(u - 3)
            pe.wait_ge(s_ev, N_IN)
            decode()
            pe.wait_ge(s_h, 1)
            pe.wait_ge(s_dend, 2)
            tile_scores(0)
            chunk_kv(0)
            for s in range(NCH):
                b = s // CPT
                if s % CPT == 4 and b + 1 < NTILE:
                    tile_scores(b + 1)
                if s + 1 < NCH:
                    chunk_kv(s + 1)
                if s % CPT == 0:
                    tile_out(b)
                chunk_out(s)
                if 3 <= s - NPC < 7:
                    head_sum(0, s - NPC - 3)
            for h in range(4):
                head_sum(1, h)
            for i in range(N_OUT):
                if i >= 2:
                    pe.wait_ge(s_res, i - 1)
                proj(T_OUT + i, i == 0, "mix")
            norm(1)
            retrieval(0)
            gate_matrix(0)
            experts(0)
            norm(2)
            for i in range(16):
                if i >= 2:
                    if i % 2 == 0:
                        pe.wait_ge(s_u, 3 * (i // 2))
                    else:
                        pe.wait_ge(s_sg, i // 2)
                proj(T_PW1 + i, i == 0, "n2")
            for n, k in enumerate(CONV_PE):
                pe.wait_ge(s_u, 3 * (k + 1))
                for i in range(CW):
                    d = CW * n + i
                    pe.wait_ge(s_dg, d + 1)
                    T.matmul(PCV[n][:, 0, 0:NP], diag[:, d % NDIAG, :], up[:, k, i:i + NP],
                             start=(i == 0), stop=(i == CW - 1))
                    T.matmul(PCV[n][:, 1, 0:NS], diag[:, d % NDIAG, :], us[:, k, :, i:i + ST],
                             start=(i == 0), stop=(i == CW - 1)).then_inc(s_dgu, 1)
            for k in CONV_PE:
                pe.wait_ge(s_cvp[k], 1)
            for k in range(KC):
                pe.wait_ge(s_cvp[k], 1)
                for a in range(2):
                    m = T.matmul(PB[0][:, a, 0:HALF], ones, cv[:, k, a * HALF:(a + 1) * HALF],
                                 start=(k == 0), stop=(k == KC - 1))
            m.then_inc(s_ms, 1)
            for k in range(KC):
                pe.wait_ge(s_csq, k + 1)
                for a in range(2):
                    m = T.matmul(PB[1][:, a, 0:HALF], ones, hf_conv[:, k, a * HALF:(a + 1) * HALF],
                                 start=(k == 0), stop=(k == KC - 1))
            m.then_inc(s_vs, 1)
            for i in range(KC):
                if i >= 2:
                    pe.wait_ge(s_res, 8 + i - 1)
                proj(T_PW2 + i, i == 0, "ln")
            norm(3)
            retrieval(1)
            gate_matrix(1)
            experts(1)

        @block.scalar
        def _(act):
            ch = Chain(act, s_a)

            def hi(t):
                act.wait_ge(s_raw[t % 2], 16 * (t // 2 + 1))
                if t >= SLOTS:
                    act.wait_ge(s_used, t - SLOTS + 1)
                A.activation(ring_hi[:, t % SLOTS, :], raw[t % 2][:], ACT.Copy).then_inc(s_hi, 1)

            def norm(n):
                for k in range(KC):
                    wait_x(act, n, k)
                    A.activation(HF[n][:, k, :], xt[:, k, :], ACT.Square).then_inc(s_sq, 1)
                act.wait_ge(s_sum, n + 1)
                A.activation(tok2(root[:, :]), both(SUMS[n]), ACT.Sqrt, bias=eps, scale=1.0 / D)\
                    .then_inc(s_root, 1)
                for k in range(KC):
                    act.wait_ge(s_hf, 8 * n + k + 1)
                    A.activation(hh[:, k, :], HF[n][:, k, :], ACT.Copy).then_inc(s_hh, 1)

            def evac(t, out, fn=ACT.Copy):
                act.wait_ge(s_used, t + 1)
                A.activation(tok2(out), both(PA[t % 2]), fn).then_inc(s_ev, 1)

            def attn_exp(u):
                b = u % 2
                act.wait_ge(s_nm, u + 1)
                for g in range(2):
                    ch.done(A.activation(sm[b][:, g, :], sm[b][:, g, :], ACT.Exp, bias=st8[:, b, 2 + g:3 + g],
                                         accum_out=st8[:, b, 6 + g:7 + g]))
                A.activation(st8[:, b, 8:10], st8[:, b, 4:6], ACT.Exp).then_inc(s_pe, 1)

            def attn_pT(u):
                act.wait_ge(s_t, u + 1)
                if u >= 2:
                    act.wait_ge(s_o, u - 1)
                A.activation(pT[u % 2], PB[1][:, 0, :].rearrange("p (a q) -> p a q", a=4), ACT.Copy)\
                    .then_inc(s_pt, 1)

            def attn_out(u):
                blk, j = divmod(u, 4)
                act.wait_ge(s_o, u + 1)
                A.activation(zq[:, j, blk * P:(blk + 1) * P], PB[1][:, 1, 0:P], ACT.Copy)\
                    .then_inc(s_oe, 1)

            def onehots(l, n, q):
                e = (NT // 8) * l + n * 16 + q
                t = n * P + 8 * q
                k = act_tokens(n, q)
                for i in range(k):
                    ch.done(A.activation(dist[:, e % 2, i, :], iota, ACT.Abs, scale=-1.0,
                                         bias=slT[:, 1, t + i:t + i + 1]))
                ch.sync()
                if n * 16 + q >= 2:
                    act.wait_ge(s_gm, e - 1)
                A.activation(oh2[:, e % 2, 0:k, :], dist[:, e % 2, 0:k, :], ACT.Relu, scale=-1.0,
                             bias=ones[:, 0:1]).then_inc(s_oha, 1)

            def retrieval(l):
                norm(1 if l == 0 else 3)
                for i in range(N_WQ):
                    t = T_WQ[l] + i
                    if i >= 2:
                        act.wait_ge(s_sc, N_WQ * l + i - 1)
                    if t + LOOK < T_WQ[l] + N_WQ:
                        hi(t + LOOK)
                    evac(t, qh[:, i % 2, :])
                select_exp(l, 0)
                for n in range(NTILE):
                    R = ROWS[n]
                    act.wait_ge(s_selT, NTILE * l + n + 1)
                    A.activation(slT[:, :, n * P:n * P + R],
                                 PB[0][:, 0, 0:3 * P].rearrange("p (i r) -> p i r", i=3)[:, :, 0:R], ACT.Copy)\
                        .then_inc(s_slT, 1)
                    act.wait_ge(s_slT, NTILE * l + n + 1)
                    onehots(l, n, 0)
                    to = stage if n < NBLK else stage_s
                    for q in range(R // 8):
                        e = (NT // 8) * l + n * 16 + q
                        if q + 1 < R // 8:
                            onehots(l, n, q + 1)
                        if q % 8 == 0 and 1 <= n < NBLK:
                            act.wait_ge(s_gw[q // 8], 32 * ((NTILE - q // 8) * l + n))
                        act.wait_ge(s_gm, e + 1)
                        A.activation(to[:, :, 8 * q:8 * q + 8].rearrange("p k t -> p t k"),
                                     PA[e % 2][:, :, :].rearrange("p a (t k) -> p (a t) k", t=4), ACT.Copy)\
                            .then_inc(s_gs, 1)
                        if q == 8:
                            write_gates(l, n, 0, 64)
                            if n + 1 < NTILE:
                                select_exp(l, n + 1)
                    if n < NBLK:
                        write_gates(l, n, 64, 128)
                    else:
                        write_gates(l, n, 0, NS)
                act.wait_ge(s_gw[0], 32 * (NTILE * l + NBLK))
                act.wait_ge(s_gw[1], 32 * NBLK * (l + 1))

            def select_exp(l, n):
                R = ROWS[n]
                act.wait_ge(s_gx, NTILE * l + n + 1)
                A.activation(sel[0:R, 2, :, :], r16[0:R, :, :], ACT.Exp).then_inc(s_ge, 1)

            def write_gates(l, n, a, b):
                act.wait_ge(s_gs, (NT // 8) * l + n * 16 + b // 8)
                src = stage if n < NBLK else stage_s
                for i in range(2):
                    act.dma_start(gdram[l, 64 * i:64 * i + 64, :, n * P + a:n * P + b].rearrange("k p t -> p k t"),
                                  src[:, 64 * i:64 * i + 64, a:b]).then_inc(s_gw[a // 64], 16)

            def experts(l):
                t0, b_e = T_EXP[l], NKEY * l

                def load_gate(slot, e):
                    act.dma_start(gt[:, slot, :], gdram[l, bass.ds(e, 1)].rearrange("a p n -> (a p) n")
                                  if not isinstance(e, int) else gdram[l, e]).then_inc(s_gld[slot], 16)

                def hi_at(slot, buf, n_loaded, used):
                    act.wait_ge(s_raw[buf], n_loaded)
                    act.wait_ge(s_used, used)
                    A.activation(ring_hi[:, slot, :], raw[buf][:], ACT.Copy).then_inc(s_hi, 1)

                def hi_rel(t, k):
                    u = t0 + 1 + k
                    hi_at(u % SLOTS, u % 2, loads(t, k), t + k - SLOTS + 1)

                def loads(t, k):
                    odd = (t0 + 1 + k) % 2
                    return (t + (k - odd)) * 8 + 16

                def gelu(e, par_e, t_used):
                    act.wait_ge(s_used, t_used)
                    A.activation(tok2(ga[:, par_e, :]), both(PA[par_e]), ACT.Gelu).then_inc(s_ga, 1)

                def split(e, slot, ws, load=True):
                    act.wait_ge(s_w, b_e + e + 1)
                    if load:
                        load_gate(slot, e + GRP)
                    A.activation(wh[:, ws, :], ga[:, slot % 2, :], ACT.Copy).then_inc(s_wh, 1)

                def group(g, par_, last=False):
                    t = t0 + 1 + 8 * g
                    n_u = 3 if last else 4
                    ahead = [k for k in range(n_u, n_u + 4)]
                    hi_rel(t, ahead[0])
                    hi_rel(t, ahead[1])
                    for j in range(1, n_u + 1):
                        e = 4 * g + j
                        act.wait_ge(s_wl, b_e + e - 1)
                        gelu(e, j % 2, t + j)
                        if j == 1:
                            hi_rel(t, ahead[2])
                        split(e, j % 4, (j % 4) if j % 4 else (0 if par_ else 4), not last)
                        if j == 1:
                            hi_rel(t, ahead[3])
                        if not last and j >= 2:
                            for k in {2: (8,), 3: (9,), 4: (10, 11)}[j]:
                                hi_rel(t, k)

                for k in range(LOOK + 1):
                    hi(t0 + k)
                act.wait_ge(s_gw[0], 32 * NTILE * (l + 1))
                for i in range(GRP):
                    load_gate(i, i)
                gelu(0, 0, t0 + 1)
                split(0, 0, 0)
                with act.Fori(0, NG // 2 - 1) as i:
                    for v in range(2):
                        g = 2 * i + v
                        group(g, v)
                t = t0 + 1 + 8 * (NG - 2)
                hi_rel(t, 4)
                hi_rel(t, 5)
                for j in range(1, 5):
                    e = 4 * (NG - 2) + j
                    act.wait_ge(s_wl, b_e + e - 1)
                    gelu(e, j % 2, t + j)
                    if j == 1:
                        hi_rel(t, 6)
                    split(e, j % 4, (j % 4) if j < 4 else 4, e + GRP < NKEY)
                    if j == 1:
                        hi_rel(t, 7)
                    if j >= 2:
                        hi_rel(t, 6 + j)
                group(NG - 1, 1, True)

            act.dma_start(par[:], params).then_inc(s_par, 16)
            act.dma_start(con[:], consts).then_inc(s_par, 16)
            act.dma_start(mc[:], mconsts).then_inc(s_mc, 16)
            act.dma_start(kwin_s[:, 0:WIN - ST, :], kvcache_n[0, :, ST:WIN, :]).then_inc(s_out, 16)
            act.dma_start(vwin_s[:, 0:WIN - ST, :], kvcache_n[1, :, ST:WIN, :]).then_inc(s_out, 16)
            for t in range(LOOK):
                hi(t)
            act.wait_ge(s_par, 32)
            act.wait_ge(s_eps, 1)
            norm(0)
            for m in range(N_IN):
                if m + LOOK < N_IN:
                    hi(m + LOOK)
                if m < 5:
                    act.wait_ge(s_used, m + 1)
                    if m >= 2:
                        act.wait_ge(s_qsum, m - 1)
                    ch.done(A.activation(tok2(zq[:, m, :]), both(PA[m % 2]), ACT.Copy))
                    A.activation(tok2(sqz[m % 2]), both(PA[m % 2]), ACT.Square).then_inc(s_ev, 1)
                elif m == 5:
                    evac(m, vT[:, :])
                elif m < 10:
                    evac(m, gates[:, m - 6, :])
                elif m < 18:
                    evac(m, gates[:, m - 6, :], ACT.Silu)
                else:
                    evac(m, gates[:, m - 6, :])
                if 1 <= m <= 5:
                    act.wait_ge(s_qsum, m)
                    if m >= 2:
                        act.wait_ge(s_qn, m - 1)
                    A.activation(tok2(rt), both(PB[0]), ACT.Sqrt, bias=eps, scale=1.0 / HD).then_inc(s_qroot, 1)
                if m == 7:
                    act.wait_ge(s_vt, 1)
                    A.activation(vtok[:, 1:5, :], PB[0][:, 0, :].rearrange("p (b f) -> p b f", b=4), ACT.Copy)\
                        .then_inc(s_vev, 1)
                    ch.done(A.activation(kvo[:, 0, :], PB[0][:, 1, 0:P], ACT.Copy))
                    A.activation(kvo[0:NS, 1:3, :],
                                 PB[0][0:NS, 1, P:3 * P].rearrange("p (i f) -> p i f", i=2), ACT.Copy)\
                        .then_inc(s_vev, 1)
                    act.wait_ge(s_vev, 2)
                    ch.sync()
                    act.dma_start(kwin_p, kvo[:, 0, :]).then_inc(s_out, 16)
                    act.dma_start(vwin_p, vtok[:, 4, :]).then_inc(s_out, 16)
                    act.dma_start(kwin_s[:, WIN - ST:WIN, :], kvo[0:NS, 1, :]).then_inc(s_out, 16)
                    act.dma_start(vwin_s[:, WIN - ST:WIN, :], kvo[0:NS, 2, :]).then_inc(s_out, 16)
                if m >= 8:
                    for u in (2 * (m - 8), 2 * (m - 8) + 1):
                        if u < 16:
                            attn_exp(u)
                        if 0 <= u - 2 < 16:
                            attn_pT(u - 2)
                        if 0 <= u - 3 < 16:
                            attn_out(u - 3)

            act.wait_ge(s_ev, N_IN)
            act.wait_ge(s_used, N_IN)
            A.activation(hT1[:, :, :], gates[:, 0:4, :], ACT.Sigmoid).then_inc(s_ha, 1)
            A.activation(hK[:, :, :], gates[:, 0:4, :], ACT.Sigmoid, scale=-1.0).then_inc(s_ha, 1)
            act.wait_ge(s_lbx, 2)
            A.activation(small[:, 28:36], small[:, 16:24], ACT.Exp).then_inc(s_lb, 1)
            act.wait_ge(s_ds, 1)
            A.activation(vnew[:, :, :], PA[0][0:ST, :, :].rearrange("p a (b f) -> p (a b) f", b=4), ACT.Copy)\
                .then_inc(s_dv, 1)
            act.wait_ge(s_dnm, 1)
            for c in range(2):
                ch.done(A.activation(pd[:, c, :], pd[:, c, :], ACT.Exp, bias=st8[:, 0, 2 + c:3 + c],
                                     accum_out=st8[:, 0, 6 + c:7 + c]))
            A.activation(st8[:, 0, 8:10], st8[:, 0, 4:6], ACT.Exp).then_inc(s_de, 1)
            act.wait_ge(s_dt, 1)
            ch.done(A.activation(pdT[:, :, :], PB[1][:, 0, 0:2 * P].rearrange("p (c q) -> p c q", c=2), ACT.Copy))
            ch.sync()
            act.wait_ge(s_dv, 1)
            A.activation(pdN[:, :, :], PB[1][0:ST, 0, 2 * P:4 * P].rearrange("p (c q) -> p c q", c=2), ACT.Copy)\
                .then_inc(s_dpt, 1)
            act.wait_ge(s_do, 1)
            for g in range(2):
                r = slice(64 * g, 64 * g + 64)
                o = PB[1][r, 1, 0:256].rearrange("p (b g r t) -> p g r b t", b=8, g=2, r=4)[:, g]
                A.activation(zq[r, 0:4, NP:NT].rearrange("p r (b t) -> p r b t", b=8), o, ACT.Copy)\
                    .then_inc(s_dend, 1)
            act.wait_ge(s_hd, 1)
            A.activation(hT1[:, :, :], hT1[:, :, :], ACT.Ln).then_inc(s_ha, 1)
            act.wait_ge(s_hd, 2)
            A.activation(hT2[:, :, :], hT1[:, :, :], ACT.Exp).then_inc(s_ha, 1)
            act.wait_ge(s_hd, 3)
            A.activation(hT2[:, :, :], hT1[:, :, :], ACT.Exp, scale=-1.0).then_inc(s_ha, 1)
            act.wait_ge(s_hd, 4)
            A.activation(hT2[:, :, :], gates[:, 0:4, :], ACT.Exp).then_inc(s_ha, 1)
            act.wait_ge(s_hd, 5)
            A.activation(hT2[:, :, :], hT1[:, :, :], ACT.Exp).then_inc(s_ha, 1)
            ch.done(A.activation(hD[:, :, 0:NPC],
                                 gates[:, 0:4, 0:NP].rearrange("p h (c t) -> p h c t", t=16)[:, :, :, 15], ACT.Exp))
            ch.done(A.activation(hD[:, :, NPC:NCH],
                                 gates[:, 0:4, NP:NT].rearrange("p h (c t) -> p h c t", t=ST)[:, :, :, ST - 1],
                                 ACT.Exp))
            ch.sync()
            A.activation(small[:, 1:2], small[:, 0:1], ACT.Copy).then_inc(s_ha, 1)
            act.wait_ge(s_dend, 2)
            for h in range(4):
                A.activation(hh[:, h, :], zq[:, h, :], ACT.Copy).then_inc(s_hh, 1)
            def tile_out(b):
                R = ROWS[b]
                act.wait_ge(s_oc, CPT * (b + 1))
                A.activation(hO[:, :, b * P:b * P + R],
                             PB[0][:, b % 2, :].rearrange("p (h t) -> p h t", h=4)[:, :, 0:R], ACT.Copy)\
                    .then_inc(s_oce, 1)

            def squares(i):
                a, b = HPART[i]
                act.wait_ge(s_oce, NBLK + i)
                for h in range(4):
                    A.activation(hK[:, h, a:b], hO[:, h, a:b], ACT.Square).then_inc(s_hsq, 1)

            def head_root(i, h):
                a, b = HPART[i]
                act.wait_ge(s_hs, 4 * i + h + 1)
                A.activation(hQ1[:, h, a:b], PA[1][:, h % 2, 0:b - a], ACT.Sqrt, bias=eps, scale=1.0 / P)\
                    .then_inc(s_hr, 1)

            for s in range(NCH):
                b, c = divmod(s, CPT)
                R = ROWS[b]
                if c == 0:
                    act.wait_ge(s_tr, b + 1)
                    if b >= 2:
                        act.wait_ge(s_oc, CPT * (b - 1))
                    A.activation(vt[b % 2][0:R, :, :],
                                 PA[b % 2][0:R, 1, :].rearrange("p (h f) -> p h f", h=4), ACT.Copy)\
                        .then_inc(s_vtile, 1)
                if s >= 2:
                    act.wait_ge(s_kv, s - 1)
                A.activation(km[s % 2][0:R, :, :], PA[b % 2][0:R, 0, :].rearrange("p (h f) -> p h f", h=4),
                             ACT.Copy, scale=mcc("rows" if b < NBLK else "rows_s")[0:R, c:c + 1])\
                    .then_inc(s_km, 1)
                if c == 1 and b >= 1:
                    tile_out(b - 1)
                if c == 1 and b == NBLK:
                    squares(0)
                if s - NPC >= 4:
                    head_root(0, s - NPC - 4)
            tile_out(NTILE - 1)
            squares(1)
            for h in range(4):
                head_root(1, h)
            for t in range(T_OUT, T_OUT + 2):
                hi(t)
            for h in range(4):
                act.wait_ge(s_mixf, 4 + h + 1)
                A.activation(hh[:, 4 + h, :], hO[:, h, :], ACT.Copy).then_inc(s_hh, 1)
            act.wait_ge(s_hl, 16)
            for t in range(T_OUT + 2, T_OUT + LOOK):
                hi(t)
            for i in range(LOOK, N_OUT):
                hi(T_OUT + i)
            act.wait_ge(s_out, 16 * 6)
            for t in range(T_WQ[0], T_WQ[0] + LOOK):
                hi(t)
            retrieval(0)
            experts(0)
            for t in range(T_PW1, T_PW1 + LOOK):
                hi(t)
            norm(2)
            for i in range(16):
                if T_PW1 + LOOK + i < T_PW2 + KC:
                    hi(T_PW1 + LOOK + i)
                if i % 2:
                    m = i // 2
                    act.wait_ge(s_used, T_PW1 + i + 1)
                    if m >= 2:
                        act.wait_ge(s_u, 3 * (m - 1))
                    A.activation(tok2(sg[:, m % 2, :]), both(PA[(T_PW1 + i) % 2]), ACT.Sigmoid,
                                 bias=pc("b1", 8 + m)).then_inc(s_sg, 1)
                if i == 7 or i == 15:
                    for d in (range(0, NDIAG) if i == 7 else range(NDIAG, CW * len(CONV_PE))):
                        if d >= NDIAG:
                            act.wait_ge(s_dgu, d - NDIAG + 1)
                        A.activation(diag[:, d % NDIAG, :], ident, ACT.Copy,
                                     scale=pc("wdw", CW * CONV_PE[d // CW] + d % CW)).then_inc(s_dg, 1)
            for n, k in enumerate(CONV_PE):
                act.wait_ge(s_dgu, CW * (n + 1))
                ch.done(A.activation(cv[:, k, 0:NP], PCV[n][:, 0, 0:NP], ACT.Identity, bias=pc("bdw", k)))
                A.activation(cv[:, k, NP:NT], PCV[n][:, 1, 0:NS], ACT.Identity, bias=pc("bdw", k))\
                    .then_inc(s_cvp[k], 1)
            act.wait_ge(s_u, 24)
            act.dma_start(cb_p.rearrange("(k p) n -> p k n", p=P), up[:, :, NP:NP + CW - 1]).then_inc(s_out, 16)
            for k in range(KC):
                act.dma_start(cb_s[k * P:(k + 1) * P], us[:, k, :, ST:ST + CW - 1]).then_inc(s_out, 16)
            for k in range(KC):
                act.wait_ge(s_cen, k + 1)
                A.activation(hf_conv[:, k, :], cv[:, k, :], ACT.Square).then_inc(s_csq, 1)
            act.wait_ge(s_vs, 1)
            A.activation(tok2(root[:, :]), both(PB[1]), ACT.Sqrt, bias=eps, scale=1.0 / D).then_inc(s_cr, 1)
            for k in range(KC):
                act.wait_ge(s_ln, k + 1)
                A.activation(cv[:, k, :], cv[:, k, :], ACT.Silu, bias=pc("lnb", k)).then_inc(s_si, 1)
            for k in range(KC):
                act.wait_ge(s_si, k + 1)
                A.activation(hh[:, k, :], cv[:, k, :], ACT.Copy).then_inc(s_hh, 1)
            for t in range(T_PW1 + LOOK + 16, T_PW2 + KC):
                hi(t)
            act.wait_ge(s_out, 16 * 15)
            for t in range(T_WQ[1], T_WQ[1] + LOOK):
                hi(t)
            retrieval(1)
            experts(1)
            act.wait_ge(s_ya, 16 * NG)
            act.dma_start(yT.rearrange("(k p) n -> p k n", p=P), xt[:]).then_inc(s_out, 16)
            act.wait_ge(s_out, 16 * (2 + 4 + 9 + 1))

        @block.vector
        def _(dve):
            ch = Chain(dve, s_v)

            def norm(n):
                dve.wait_ge(s_root, n + 1)
                ch.step(V.reciprocal(root[:, :], root[:, :]))
                for k in range(KC + 2):
                    if k < KC:
                        V.scalar_tensor_tensor(out=HF[n][:, k, :], in0=xt[:, k, :], scalar=pc(GN[n], k),
                                               in1=root[:, :], op0=ALU.mult, op1=ALU.mult).then_inc(s_hf, 1)
                    if k >= 2:
                        lo_parts([HF[n][:, k - 2, :]], f"n{n}", k - 2)

            def lo_parts(src, event, k0=0):
                for k, a in enumerate(src):
                    dve.wait_ge(s_hh, 8 * H_EVENT[event] + k0 + k + 1)
                    V.tensor_tensor(hl[:, k0 + k, :], a, hh[:, k0 + k, :].bitcast(F32), ALU.subtract)\
                        .then_inc(s_hl, 1)

            def softmax_a(u):
                b = u % 2
                blk, j = divmod(u, 4)
                dve.wait_ge(s_s, u + 1)
                if u >= 2:
                    dve.wait_ge(s_t, u - 1)
                mask = mcc("band0" if blk == 0 else "band")
                V.scalar_tensor_tensor(out=sm[b], in0=PB[0][:, b, :].rearrange("p (g k) -> p g k", g=2),
                                       scalar=SCALE, in1=mask.unsqueeze(1).to_broadcast([P, 2, 256]),
                                       op0=ALU.mult, op1=ALU.add).then_inc(s_sm, 1)
                dve.wait_ge(s_sm, u + 1)
                ch.step(V.tensor_reduce(st8[:, b, 0:2], sm[b], X, ALU.max))
                ch.step(V.tensor_tensor(st8[:, b, 0:2], st8[:, b, 0:2], pc("sink", 2 * j, 2), ALU.max))
                ch.step(V.tensor_scalar(st8[:, b, 2:4], st8[:, b, 0:2], -1.0, None, ALU.mult))
                V.tensor_tensor(st8[:, b, 4:6], pc("sink", 2 * j, 2), st8[:, b, 2:4], ALU.add).then_inc(s_nm, 1)

            def softmax_b(u):
                b = u % 2
                dve.wait_ge(s_pe, u + 1)
                ch.step(V.tensor_tensor(st8[:, b, 10:12], st8[:, b, 6:8], st8[:, b, 8:10], ALU.add))
                ch.step(V.reciprocal(st8[:, b, 12:14], st8[:, b, 10:12]))
                ch.step(V.tensor_scalar(sm[b][:, 0, :], sm[b][:, 0, :], st8[:, b, 12:13], None, ALU.mult))
                V.tensor_scalar(sm[b][:, 1, :], sm[b][:, 1, :], st8[:, b, 13:14], None, ALU.mult).then_inc(s_p, 1)

            def retrieval(l):
                norm(1 if l == 0 else 3)
                for q in range(N_WQ):
                    dve.wait_ge(s_sc, N_WQ * l + q + 1)
                    src = [PB[q % 2][0:ROWS[n], n // 4, (n % 4) * P:(n % 4 + 1) * P] for n in range(NTILE)]
                    val = [sv[0:ROWS[n], n, q, :] for n in range(NTILE)]
                    idx = [si[0:ROWS[n], n, q, :] for n in range(NTILE)]
                    tmp = [sc2[0:ROWS[n], n, :] for n in range(NTILE)]
                    for n in range(NTILE):
                        ch.done(V.max(val[n][:, 0:8], src[n]))
                    ch.sync()
                    for n in range(NTILE):
                        ch.done(V.max_index(idx[n][:, 0:8], val[n][:, 0:8], src[n]))
                    for n in range(NTILE):
                        m = V.match_replace(out=tmp[n], in_to_replace=val[n][:, 0:8], in_values=src[n],
                                            imm_value=-3e38)
                        if n < NTILE - 1:
                            ch.done(m)
                    m.then_inc(s_scf, 1)
                    ch.sync()
                    dve.wait_ge(s_scf, N_WQ * l + q + 1)
                    for n in range(NTILE):
                        ch.done(V.max(val[n][:, 8:16], tmp[n]))
                    ch.sync()
                    for n in range(NTILE):
                        ch.done(V.max_index(idx[n][:, 8:16], val[n][:, 8:16], tmp[n]))
                    ch.sync()
                    if q % 2:
                        head_best(l, 0, q // 2)
                for part in range(4, N_SEL):
                    select(l, 0, part)
                for n in range(NTILE):
                    onehots(l, n)

            def head_best(l, n, h):
                R = ROWS[n]
                val = sv[0:R, n, 2 * h:2 * h + 2, :]
                if h == 0 and l >= 1:
                    dve.wait_ge(s_ge, NTILE * l)
                for a in range(8):
                    w = CAND_W[a]
                    ch.done(V.tensor_tensor(cand[0:R, h, CAND_AT[a]:CAND_AT[a] + w], val[:, 1, 0:w],
                                            val[:, 0, a:a + 1].to_broadcast([R, w]), ALU.add))
                ch.step(V.tensor_tensor(cand[0:R, h, CAND_AT[8]:NCAND], val[:, 0, 8:16],
                                        val[:, 1, 0:1].to_broadcast([R, 8]), ALU.add))
                ch.step(V.max(fv[0:R, h, 0:8], cand[0:R, h, :]))
                ch.done(V.max_index(fi[0:R, h, 0:8], fv[0:R, h, 0:8], cand[0:R, h, :]))
                ch.step(V.match_replace(out=cand2[0:R, h, :], in_to_replace=fv[0:R, h, 0:8],
                                        in_values=cand[0:R, h, :], imm_value=-3e38))
                ch.step(V.max(fv[0:R, h, 8:16], cand2[0:R, h, :]))
                ch.done(V.max_index(fi[0:R, h, 8:16], fv[0:R, h, 8:16], cand2[0:R, h, :]))

            def select(l, n, part):
                R = ROWS[n]
                val = sv[0:R, n, :, :].rearrange("p (h s) k -> p h s k", s=2)
                sidx = sif[0:R, :, :].rearrange("p (h s) k -> p h s k", s=2)
                ch.sync()
                if part == 0:
                    ch.done(V.tensor_copy(sif[0:R, :, :], si[0:R, n, :, :]))
                    for a in range(8):
                        w = CAND_W[a]
                        ch.done(V.tensor_tensor(cand[0:R, :, CAND_AT[a]:CAND_AT[a] + w],
                                                val[:, :, 1, 0:w],
                                                val[:, :, 0, a:a + 1].to_broadcast([R, 8, w]), ALU.add))
                    ch.done(V.tensor_tensor(cand[0:R, :, CAND_AT[8]:NCAND], val[:, :, 0, 8:16],
                                            val[:, :, 1, 0:1].to_broadcast([R, 8, 8]), ALU.add))
                elif part == 1:
                    for h in range(8):
                        ch.done(V.max(fv[0:R, h, 0:8], cand[0:R, h, :]))
                elif part == 2:
                    for h in range(8):
                        ch.done(V.max_index(fi[0:R, h, 0:8], fv[0:R, h, 0:8], cand[0:R, h, :]))
                        ch.done(V.match_replace(out=cand2[0:R, h, :], in_to_replace=fv[0:R, h, 0:8],
                                                in_values=cand[0:R, h, :], imm_value=-3e38))
                elif part == 3:
                    for h in range(8):
                        ch.done(V.max(fv[0:R, h, 8:16], cand2[0:R, h, :]))
                elif part == 4:
                    if n == 0:
                        ch.done(V.tensor_copy(sif[0:R, :, :], si[0:R, n, :, :]))
                    else:
                        for h in range(8):
                            ch.done(V.max_index(fi[0:R, h, 8:16], fv[0:R, h, 8:16], cand2[0:R, h, :]))
                    if n >= 1 or l >= 1:
                        dve.wait_ge(s_ge, NTILE * l + n)
                        dve.wait_ge(s_selT, NTILE * l + n)
                    V.tensor_tensor(r16[0:R, :, :], fv[0:R, :, :], fv[0:R, :, 0:1].to_broadcast([R, 8, 16]),
                                    ALU.subtract).then_inc(s_gx, 1)
                elif part == 5:
                    ch.done(V.tensor_copy(pos[0:R, :, :], fi[0:R, :, :]))
                    ch.done(V.tensor_tensor(dsi[0:R, :, :], sidx[:, :, 0, 1:16], sidx[:, :, 0, 0:15],
                                            ALU.subtract))
                elif part in (6, 7):
                    f = part - 6
                    for h in range(4):
                        m = V.tensor_tensor(ge[f][0:R, h, :, 0:15],
                                            pos[0:R, 4 * f + h, :].unsqueeze(2).to_broadcast([R, 16, 15]),
                                            cc("start")[0:R, :].unsqueeze(1).to_broadcast([R, 16, 15]),
                                            ALU.is_ge)
                        if h == 3:
                            m.then_inc(s_cmp, 1)
                    dve.wait_ge(s_cmp, 4 * (NTILE * l + n) + f + 1)
                    for h in range(4):
                        ch.done(V.tensor_tensor(tm2[f][0:R, h, :, 0:15], ge[f][0:R, h, :, 0:15],
                                                cc("dstart")[0:R, :].unsqueeze(1).to_broadcast([R, 16, 15]),
                                                ALU.mult))
                elif part in (8, 10):
                    f = (part - 8) // 2
                    hs = slice(4 * f, 4 * f + 4)
                    dve.wait_ge(s_prd, 4 * (NTILE * l + n) + f + 1)
                    ch.done(V.tensor_reduce(sel[0:R, 0, hs, :], tm[f][0:R, :, :, 0:15], X, ALU.add))
                    ch.done(V.tensor_reduce(sel[0:R, 1, hs, :], tm2[f][0:R, :, :, 0:15], X, ALU.add))
                elif part in (9, 11):
                    f = (part - 9) // 2
                    hs = slice(4 * f, 4 * f + 4)
                    ch.step(V.tensor_tensor(pos[0:R, hs, :], pos[0:R, hs, :], sel[0:R, 1, hs, :],
                                            ALU.subtract))
                    for h in range(4):
                        m = V.tensor_tensor(ge[f][0:R, h, :, :],
                                            pos[0:R, 4 * f + h, :].unsqueeze(2).to_broadcast([R, 16, 16]),
                                            iota[0:R, 0:16].unsqueeze(1).to_broadcast([R, 16, 16]),
                                            ALU.is_equal)
                    m.then_inc(s_cmp, 1)
                elif part in (12, 13):
                    f = part - 12
                    dve.wait_ge(s_prd, 4 * (NTILE * l + n) + f + 3)
                    ch.done(V.tensor_reduce(sel[0:R, 1, 4 * f:4 * f + 4, :], tm[f][0:R, :, :, :], X, ALU.add))
                else:
                    ch.done(V.tensor_tensor(sel[0:R, 0, :, :], sel[0:R, 0, :, :],
                                            sidx[:, :, 0, 0:1].to_broadcast([R, 8, 16]), ALU.add))
                    dve.wait_ge(s_ge, NTILE * l + n + 1)
                    ch.step(V.tensor_reduce(r8[0:R, 0, :], sel[0:R, 2, :, :], X, ALU.add))
                    ch.step(V.reciprocal(r8[0:R, 1, :], r8[0:R, 0, :]))
                    V.tensor_tensor(sel[0:R, 2, :, :], sel[0:R, 2, :, :],
                                    r8[0:R, 1, :].unsqueeze(2).to_broadcast([R, 8, 16]), ALU.mult)\
                        .then_inc(s_sel, 1)

            def onehots(l, n):
                dve.wait_ge(s_slT, NTILE * l + n + 1)
                for q in range(ROWS[n] // 8):
                    e = (NT // 8) * l + n * 16 + q
                    t = n * P + 8 * q
                    if n * 16 + q >= 2:
                        dve.wait_ge(s_gm, e - 1)
                    V.tensor_tensor(oh1[:, e % 2, :, :], iota.unsqueeze(1).to_broadcast([P, 8, P]),
                                    slT[:, 0, t:t + 8].unsqueeze(2).to_broadcast([P, 8, P]), ALU.is_equal)                        .then_inc(s_eq, 1)
                    k = act_tokens(n, q)
                    V.tensor_tensor(oh2[:, e % 2, k:8, :], iota.unsqueeze(1).to_broadcast([P, 8 - k, P]),
                                    slT[:, 1, t + k:t + 8].unsqueeze(2).to_broadcast([P, 8 - k, P]),
                                    ALU.is_equal).then_inc(s_oh, 1)
                    if 1 <= q <= N_SEL and n + 1 < NTILE:
                        select(l, n + 1, q - 1)

            def experts(l):
                t0, b_e = T_EXP[l], NKEY * l

                def gate(e, par_e, slot, n_loads, ws):
                    dve.wait_ge(s_ga, b_e + e + 1)
                    dve.wait_ge(s_gld[slot], n_loads)
                    V.tensor_tensor(ga[:, par_e, :], ga[:, par_e, :], gt[:, slot, :], ALU.mult).then_inc(s_w, 1)
                    dve.wait_ge(s_wh, b_e + e + 1)
                    V.tensor_tensor(wl[:, ws, :], ga[:, par_e, :], wh[:, ws, :].bitcast(F32), ALU.subtract)\
                        .then_inc(s_wl, 1)

                def group(g, par_, last=False):
                    t = t0 + 1 + 8 * g
                    n_u = 3 if last else 4
                    for j in range(1, n_u + 1):
                        gg = g if j < 4 else g + 1
                        gate(4 * g + j, j % 2, j % 4, 16 * (NG * l + 1) + 16 * gg,
                             j % 4 if j < 4 else (0 if par_ else 4))
                    for c in range(KC):
                        if c < KC - 1:
                            dve.wait_ge(s_y, (KC - 1) * (NG * l) + (KC - 1) * g + c + 1)
                        else:
                            dve.wait_ge(s_used, t + n_u + GRP)
                        V.tensor_tensor(tok2(xt[:, c, :]), tok2(xt[:, c, :]), both(PB[c % 2]), ALU.add)\
                            .then_inc(s_ya, 1)

                gate(0, 0, 0, 16 * (NG * l + 1), 0)
                with dve.Fori(0, NG // 2 - 1) as i:
                    group(2 * i, 0)
                    group(2 * i + 1, 1)
                group(NG - 2, 0)
                group(NG - 1, 1, True)

            V.memset(small[:], 0.0).then_inc(s_v, 1)
            ch.n += 1
            ch.sync()
            V.memset(small[:, 0:1], EPS).then_inc(s_eps, 1)
            V.memset(krp[:, 0:P], 0.0).then_inc(s_pad, 1)
            ch.step(V.memset(krz[:, :, :], 0.0))
            V.memset(vtok[:, 0, :], 0.0).then_inc(s_pad, 1)
            dve.wait_ge(s_par, 32)
            dve.wait_ge(s_x, 16)
            norm(0)
            dve.wait_ge(s_mc, 16)
            for m in range(1, 7):
                if m <= 5:
                    j = m - 1
                    dve.wait_ge(s_qroot, j + 1)
                    ch.step(V.reciprocal(rt, rt))
                    V.scalar_tensor_tensor(out=zq[:, j, :], in0=zq[:, j, :], scalar=pc("gq" if j < 4 else "gk"),
                                           in1=rt, op0=ALU.mult, op1=ALU.mult).then_inc(s_qn, 1)
                if m >= 2:
                    j = m - 2
                    dve.wait_ge(s_qrot, j + 1)
                    ch.done(V.tensor_tensor(tok2(rt2), both(PB[1]), tok2(mcc("sin")), ALU.mult))
                    ch.step(V.tensor_tensor(zq[:, j, :], zq[:, j, :], mcc("cos"), ALU.mult))
                    out = zq[:, j, :] if j < 4 else krp[:, P:P + NT]
                    V.tensor_tensor(out, zq[:, j, :], rt2, ALU.add).then_inc(s_qr, 1)
            dve.wait_ge(s_qr, 5)
            for g in range(2):
                r = slice(64 * g, 64 * g + 64)
                V.tensor_copy(krz[r, g, P:P + NT], krp[r, P:P + NT]).then_inc(s_pad, 1)
            for u in range(17):
                if u < 16:
                    softmax_a(u)
                if u >= 1:
                    softmax_b(u - 1)
            lb = small[:, 8:12]
            oml = small[:, 12:16]
            ch.step(V.tensor_tensor(small[:, 24:28], pc("lb1", 0, 4), pc("lb0", 0, 4), ALU.max))
            V.tensor_tensor(small[:, 16:20], pc("lb0", 0, 4), small[:, 24:28], ALU.subtract).then_inc(s_lbx, 1)
            V.tensor_tensor(small[:, 20:24], pc("lb1", 0, 4), small[:, 24:28], ALU.subtract).then_inc(s_lbx, 1)
            dve.wait_ge(s_used, N_IN)
            dve.wait_ge(s_dload, 32)
            ch.step(V.memset(qbd[:, :, :, :, :], 0.0))
            ch.done(V.tensor_copy(kcat[:, :, WIN:WIN + ST], krp[:, P + NP:P + NT].rearrange("p (b t) -> p b t", b=SB)))
            for g in range(2):
                r = slice(64 * g, 64 * g + 64)
                for j in range(4):
                    ch.done(V.tensor_copy(qbd[r, :, g, j, :], zq[r, j, NP:NT].rearrange("p (b t) -> p b t", b=SB)))
            ch.sync()
            V.memset(small[:, 2:3], 0.0).then_inc(s_dq, 1)
            dve.wait_ge(s_ds, 1)
            ch.step(V.scalar_tensor_tensor(out=pd[:, :, :], in0=PB[0][:, :, 0:WIN + ST], scalar=SCALE,
                                           in1=mcc("dec").unsqueeze(1).to_broadcast([P, 2, WIN + ST]),
                                           op0=ALU.mult, op1=ALU.add))
            st = st8[:, 0, :]
            ch.step(V.tensor_reduce(st[:, 0:2], pd[:, :, :], X, ALU.max))
            ch.step(V.tensor_scalar(st[:, 0:2], st[:, 0:2], pc("sinkd"), None, ALU.max))
            ch.step(V.tensor_scalar(st[:, 2:4], st[:, 0:2], -1.0, None, ALU.mult))
            V.tensor_scalar(st[:, 4:6], st[:, 2:4], pc("sinkd"), None, ALU.add).then_inc(s_dnm, 1)
            dve.wait_ge(s_de, 1)
            ch.step(V.tensor_tensor(st[:, 10:12], st[:, 6:8], st[:, 8:10], ALU.add))
            ch.step(V.reciprocal(st[:, 12:14], st[:, 10:12]))
            ch.step(V.tensor_scalar(pd[:, 0, :], pd[:, 0, :], st[:, 12:13], None, ALU.mult))
            V.tensor_scalar(pd[:, 1, :], pd[:, 1, :], st[:, 13:14], None, ALU.mult).then_inc(s_dp, 1)
            dve.wait_ge(s_lb, 1)
            ch.step(V.tensor_tensor(small[:, 24:28], small[:, 28:32], small[:, 32:36], ALU.add))
            ch.step(V.reciprocal(small[:, 24:28], small[:, 24:28]))
            ch.step(V.tensor_tensor(lb, small[:, 28:32], small[:, 24:28], ALU.mult))
            ch.step(V.tensor_scalar(oml, lb, -1.0, 1.0, ALU.mult, ALU.add))
            dve.wait_ge(s_ha, 2)
            for h in range(4):
                ch.done(V.tensor_scalar(hT1[:, h, :], hT1[:, h, :], oml[:, h:h + 1], lb[:, h:h + 1],
                                        ALU.mult, ALU.add))
                ch.done(V.tensor_scalar(hK[:, h, :], hK[:, h, :], oml[:, h:h + 1], None, ALU.mult))
            ch.sync()
            V.memset(small[:, 3:4], 0.0).then_inc(s_hd, 1)
            dve.wait_ge(s_ha, 3)
            dve.wait_ge(s_reset, 16)
            for h in range(4):
                ch.done(V.tensor_tensor_scan(gates[:, h, :], resm, hT1[:, h, :], 0.0, ALU.mult, ALU.add))
            ch.sync()

            def views(a, i=None):
                out = []
                for h in range(4):
                    for lo, hi_, C in ((0, NP, 16), (NP, NT, ST)):
                        v = a[:, h, lo:hi_].rearrange("p (c t) -> p c t", t=C)
                        if i is not None:
                            m = (C // 2 - 1) if i == "mid" else C - 1
                            v = v[:, :, m:m + 1].to_broadcast([P, (hi_ - lo) // C, C])
                        out.append(v)
                return out
            b = gates[:, 0:4, :]
            for o, i0, i1 in zip(views(hT1), views(b), views(b, "mid")):
                ch.done(V.tensor_tensor(o, i0, i1, ALU.subtract))
            ch.sync()
            V.tensor_scalar(hT1[:, :, :], hT1[:, :, :], -80.0, 80.0, ALU.max, ALU.min).then_inc(s_hd, 1)
            dve.wait_ge(s_ha, 4)
            V.tensor_tensor(hQ1[:, :, :], gates[:, 4:8, :], hT2[:, :, :], ALU.mult).then_inc(s_hd, 1)
            dve.wait_ge(s_ha, 5)
            V.tensor_tensor(hK1[:, :, :], hK[:, :, :], hT2[:, :, :], ALU.mult).then_inc(s_hd, 1)
            for o, i0, i1 in zip(views(hT1), views(b, "last"), views(b)):
                ch.done(V.tensor_tensor(o, i0, i1, ALU.subtract))
            dve.wait_ge(s_hd, 3)
            dve.wait_ge(s_ha, 6)
            ch.sync()
            V.tensor_tensor(gates[:, 4:8, :], gates[:, 4:8, :], hT2[:, :, :], ALU.mult).then_inc(s_hd, 1)
            dve.wait_ge(s_hd, 5)
            dve.wait_ge(s_ha, 7)
            ch.step(V.tensor_tensor(hK[:, :, :], hK[:, :, :], hT2[:, :, :], ALU.mult))
            dve.wait_ge(s_ha, 8)
            dve.wait_ge(s_t, 16)
            for a in am:
                ch.done(V.memset(a, 0.0))
            ch.sync()
            V.memset(Sb[0], 0.0).then_inc(s_S, 1)
            V.memset(small[:, 4:5], 0.0).then_inc(s_h, 1)
            lo_parts([zq[:, h, :] for h in range(4)], "mix")
            def mask(b):
                R = ROWS[b]
                dve.wait_ge(s_at, b + 1)
                if b >= 2:
                    dve.wait_ge(s_oc, CPT * (b - 2) + 1)
                if b == NBLK:
                    ch.step(V.memset(am[b % 2][0:R, :, 0:R], 0.0))
                tri = mcc("tri" if b < NBLK else "tri_s")[0:R, :].bitcast(U32)
                V.copy_predicated(am[b % 2][0:R, :, 0:R], tri.unsqueeze(1).to_broadcast([R, 4, R]),
                                  PB[0][0:R, b % 2, :].rearrange("p (h t) -> p h t", h=4)[:, :, 0:R])\
                    .then_inc(s_am, 1)

            def head_norm(i, h):
                a, b = HPART[i]
                root_h, out = hQ1[:, h, a:b], hO[:, h, a:b]
                dve.wait_ge(s_hr, 4 * i + h + 1)
                ch.step(V.reciprocal(root_h, root_h))
                ch.step(V.scalar_tensor_tensor(out=out, in0=out, scalar=pc("og"), in1=root_h,
                                               op0=ALU.mult, op1=ALU.mult))
                V.tensor_tensor(out, out, gates[:, 8 + h, a:b], ALU.mult).then_inc(s_mixf, 1)

            mask(0)
            for s in range(1, NCH + 1):
                if s >= 1:
                    q = s - 1
                    bq = q - NPC
                    dve.wait_ge(s_kv, q + 1)
                    src = Sb[q % 2] if bq < 0 else Ssm[bq % 4]
                    dst = Sb[(q + 1) % 2] if bq < 0 else src
                    if bq >= 0:
                        dve.wait_ge(s_oc, q + 1)
                    elif q >= 1:
                        dve.wait_ge(s_oc, q)
                        dve.wait_ge(s_S, q + 1)
                    for h in range(4):
                        m = V.scalar_tensor_tensor(out=dst[:, h, :], in0=src[:, h, :], scalar=hD[:, h, q:q + 1],
                                                   in1=PB[1][:, q % 2, h * P:(h + 1) * P],
                                                   op0=ALU.mult, op1=ALU.add)
                    m.then_inc(s_S, 1)
                    if q % CPT == 5 and q < NPC:
                        mask(q // CPT + 1)
                    if bq >= 4:
                        head_norm(0, bq - 4)
            for h in range(4):
                head_norm(1, h)
            lo_parts([hO[:, h, :] for h in range(4)], "mix", 4)

            def residual(t0, base):
                for i in range(KC):
                    dve.wait_ge(s_used, t0 + i + 1)
                    V.tensor_tensor(tok2(xt[:, i, :]), tok2(xt[:, i, :]), both(PA[(t0 + i) % 2]), ALU.add)\
                        .then_inc(s_res, 1)
            residual(T_OUT, 0)
            retrieval(0)
            experts(0)
            norm(2)
            ch.done(V.memset(up[:, :, 0:CW - 1], 0.0))
            dve.wait_ge(s_conv, 16 * KC)
            def glu(m):
                dve.wait_ge(s_used, T_PW1 + 2 * m + 1)
                dve.wait_ge(s_sg, m + 1)
                pa = PA[T_PW1 % 2]
                for o, i0, i1 in ((up[:, m, CW - 1:CW - 1 + HALF], pa[:, 0, 0:HALF], sg[:, m % 2, 0:HALF]),
                                  (up[:, m, CW - 1 + HALF:CW - 1 + NP], pa[:, 1, 0:NP - HALF],
                                   sg[:, m % 2, HALF:NP]),
                                  (us[:, m, :, CW - 1:CW - 1 + ST],
                                   pa[:, 1, NP - HALF:HALF].rearrange("p (b t) -> p b t", b=SB),
                                   sg[:, m % 2, NP:NT].rearrange("p (b t) -> p b t", b=SB))):
                    V.scalar_tensor_tensor(out=o, in0=i0, scalar=pc("b1", m), in1=i1,
                                           op0=ALU.add, op1=ALU.mult).then_inc(s_u, 1)

            n_glu = 0
            for grp in CONV_DVE:
                while n_glu <= max(grp):
                    glu(n_glu)
                    n_glu += 1
                dve.wait_ge(s_u, 3 * n_glu)
                ch.sync()
                at = {}
                for i in range(CW):
                    if i % 7 == 6 and n_glu < KC:
                        glu(n_glu)
                        n_glu += 1
                    for m in grp:
                        if i:
                            dve.wait_ge(s_v, at[m])
                        for a0, c0 in ((up[:, m, i:i + NP], cv[:, m, 0:NP]),
                                       (us[:, m, :, i:i + ST], cv[:, m, NP:NT].rearrange("p (b t) -> p b t", b=SB))):
                            w = pc("wdw", CW * m + i)
                            if i == 0:
                                tap = V.tensor_scalar(c0, a0, w, pc("bdw", m), ALU.mult, ALU.add)
                            else:
                                tap = V.scalar_tensor_tensor(out=c0, in0=a0, scalar=w, in1=c0,
                                                            op0=ALU.mult, op1=ALU.add)
                            if i == CW - 1 and c0.shape != cv[:, m, 0:NP].shape:
                                tap.then_inc(s_cvp[m], 1)
                            else:
                                ch.done(tap)
                        at[m] = ch.n
            dve.wait_ge(s_ms, 1)
            ch.step(V.tensor_scalar(tok2(sg[:, 0, :]), both(PB[0]), 1.0 / D, None, ALU.mult))
            for k in range(KC):
                V.tensor_tensor(cv[:, k, :], cv[:, k, :], sg[:, 0, :], ALU.subtract).then_inc(s_cen, 1)
            dve.wait_ge(s_cr, 1)
            ch.step(V.reciprocal(root[:, :], root[:, :]))
            for k in range(KC):
                V.scalar_tensor_tensor(out=cv[:, k, :], in0=cv[:, k, :], scalar=pc("lng", k), in1=root[:, :],
                                       op0=ALU.mult, op1=ALU.mult).then_inc(s_ln, 1)
            for k in range(KC):
                dve.wait_ge(s_si, k + 1)
            lo_parts([cv[:, k, :] for k in range(KC)], "ln")
            residual(T_PW2, 8)
            retrieval(1)
            experts(1)

        @block.gpsimd
        def _(pool):
            def lo(t, slot, buf):
                pool.wait_ge(s_hi, t + 1)
                nc.gpsimd.tensor_tensor(ring_lo[:, slot, :], raw[buf][:], ring_hi[:, slot, :].bitcast(F32),
                                        ALU.subtract).then_inc(s_lo, 1)

            def lo_run(a, b):
                n = (b - a) // SLOTS
                if n >= 2:
                    with pool.Fori(0, n) as i:
                        for u in range(SLOTS):
                            lo(8 * i + (a + u), (a + u) % SLOTS, (a + u) % 2)
                    a += n * SLOTS
                for t in range(a, b):
                    lo(t, t % SLOTS, t % 2)

            def gate_onehots(l):
                for part in range(N_SEL):
                    select_products(l, 0, part)
                for n in range(NTILE):
                    for q in range(ROWS[n] // 8):
                        e = (NT // 8) * l + n * 16 + q
                        t = n * P + 8 * q
                        pool.wait_ge(s_eq, e + 1)
                        nc.gpsimd.tensor_tensor(oh1[:, e % 2, :, :], oh1[:, e % 2, :, :],
                                                slT[:, 2, t:t + 8].unsqueeze(2).to_broadcast([P, 8, P]),
                                                ALU.mult).then_inc(s_ohp, 1)
                        if 1 <= q <= N_SEL and n + 1 < NTILE:
                            select_products(l, n + 1, q - 1)

            def select_products(l, n, part):
                R = ROWS[n]
                tt = nc.gpsimd.tensor_tensor
                if part in (6, 7):
                    f = part - 6
                    pool.wait_ge(s_cmp, 4 * (NTILE * l + n) + f + 1)
                    for h in range(4):
                        m = tt(tm[f][0:R, h, :, 0:15], ge[f][0:R, h, :, 0:15],
                               dsi[0:R, 4 * f + h, :].unsqueeze(1).to_broadcast([R, 16, 15]), ALU.mult)
                    m.then_inc(s_prd, 1)
                elif part in (9, 11):
                    f = (part - 9) // 2
                    pool.wait_ge(s_cmp, 4 * (NTILE * l + n) + f + 3)
                    for h in range(4):
                        m = tt(tm[f][0:R, h, :, :], ge[f][0:R, h, :, :],
                               sif[0:R, 2 * (4 * f + h) + 1, :].unsqueeze(1).to_broadcast([R, 16, 16]), ALU.mult)
                    m.then_inc(s_prd, 1)

            lo_run(0, N_IN)
            pool.wait_ge(s_used, N_IN)
            pool.dma_start(kcat[:, :, 0:WIN], kcacheT).then_inc(s_dload, 16)
            pool.dma_start(vcat[:, :, :], vcache).then_inc(s_dload, 16)
            pool.wait_ge(s_qr, 5)
            pool.dma_start(resm, reset).then_inc(s_reset, 16)
            pool.wait_ge(s_o, 16)
            def load_state(b):
                pool.dma_start(Ssm[b % 4], state_h[b].rearrange("h k v -> k h v")).then_inc(s_sl[b % 4], 16)

            for b in range(4):
                load_state(b)
            for b in range(SB):
                pool.wait_ge(s_S, 2 + NPC + b)
                pool.dma_start(hs_s[b].rearrange("h k v -> k h v"), Ssm[b % 4]).then_inc(s_so[b % 4], 16)
                if 1 <= b <= SB - 4:
                    pool.wait_ge(s_so[(b - 1) % 4], 16)
                    load_state(b + 3)
            pool.dma_start(hs_p.rearrange("h k v -> k h v"), Sb[NPC % 2]).then_inc(s_hsp, 16)
            for i in range(4):
                pool.wait_ge(s_so[i], 16 * (SB // 4))
            pool.wait_ge(s_hsp, 16)
            lo_run(T_OUT, T_OUT + N_OUT)
            pool.wait_ge(s_res, 1)
            pool.dma_start(keys[:, :, :], keysT[0]).then_inc(s_keys, 16)
            lo_run(T_WQ[0], T_WQ[0] + N_WQ)
            gate_onehots(0)
            lo_run(T_EXP[0], T_EXP[0] + N_EXP)
            pool.wait_ge(s_wl, NKEY)
            pool.wait_ge(s_used, T_EXP[0] + N_EXP)
            for k in range(KC):
                pool.dma_start(us[:, k, :, 0:CW - 1], convT[k * P:(k + 1) * P]).then_inc(s_conv, 16)
            lo_run(T_PW1, T_PW2)
            lo_run(T_PW2, T_PW2 + KC)
            pool.wait_ge(s_res, 9)
            pool.wait_ge(s_out, 16 * 15)
            pool.dma_start(keys[:, :, :], keysT[1]).then_inc(s_keys, 16)
            lo_run(T_WQ[1], T_WQ[1] + N_WQ)
            gate_onehots(1)
            lo_run(T_EXP[1], T_EXP[1] + N_EXP)


_OUTS = [("yT", (D, NT)), ("kwin_p", (P, P)), ("vwin_p", (P, P)), ("s_p", (4, P, P)), ("cb_p", (D, CW - 1)),
         ("kwin_s", (SB, WIN, P)), ("vwin_s", (SB, WIN, P)), ("s_s", (SB, 4, P, P)), ("cb_s", (D, SB, CW - 1))]


def kernel(**inputs):
    import numpy as np
    import concourse.bacc as _bacc
    from concourse import mybir as _mybir
    from concourse.bass_utils import run_bass_kernel_spmd as _run
    i = {k: np.asarray(v) for k, v in inputs.items()}
    f32 = np.float32

    def chan(v, w=1):
        return v.reshape(-1, P).T

    def tiles(w):
        return w.reshape(KC, P, -1, P).transpose(2, 1, 0, 3).reshape(-1, P, D)

    order = [h for j in range(4) for h in (j, 4 + j)]
    w_in = i["w_in0"]
    q = w_in[:, 0:512].reshape(D, 8, HD)[:, order].reshape(D, 512)
    k, v = w_in[:, 512:640], w_in[:, 640:768]
    qb, fb, ib, gb = (w_in[:, 768 + 512 * n:768 + 512 * (n + 1)] for n in range(4))
    w_out = i["w_out0"]
    wo = np.concatenate([w_out[0:512].reshape(8, HD, D)[order].reshape(512, D), w_out[512:]], 0)
    pw1 = i["conv_w_pw1"].reshape(D, 2, KC, P).transpose(0, 2, 1, 3).reshape(D, 2 * D)
    parts = [tiles(x) for x in (q, k, v, fb, qb, gb, ib, wo, i["peer_w_q"][0])]

    def expert_tiles(l):
        u = i["peer_u"][l].reshape(NKEY, P, KC, P).transpose(0, 3, 2, 1).reshape(NKEY, P, D)
        w = i["peer_v"][l].reshape(NKEY, P, D)
        out = [u[0:1]]
        for g in range(NG):
            out += [u[4 * g + 1:4 * g + 5], w[4 * g:4 * g + 4]]
        return out
    parts += expert_tiles(0)
    parts += [tiles(pw1), tiles(i["conv_w_pw2"]), tiles(i["peer_w_q"][1])]
    parts += expert_tiles(1)
    stream = np.concatenate(parts, 0)

    xT = np.concatenate([i["x_prompt"].reshape(NP, D), i["x_sample"].reshape(NS, D)], 0).T
    par = np.zeros((P, NPAR), f32)

    def put(n, a):
        par[:, PC[n][0]:PC[n][0] + PC[n][1]] = a
    for n, a in (("g_mix0", i["norm_mix_g"][0]), ("g_mix1", i["norm_mix_g"][1]), ("g_ffn0", i["norm_ffn_g"][0]),
                 ("g_ffn1", i["norm_ffn_g"][1]), ("lb0", i["hgrn_lb"][0]), ("lb1", i["hgrn_lb"][1]),
                 ("og", i["hgrn_o_norm_g"]), ("b1", i["conv_b_pw1"]), ("bdw", i["conv_b_dw"]),
                 ("lng", i["conv_ln_g"]), ("lnb", i["conv_ln_b"])):
        put(n, chan(a))
    put("gq", np.concatenate([i["attn_q_norm_g"]] * 2)[:, None])
    put("gk", np.concatenate([i["attn_k_norm_g"]] * 2)[:, None])
    put("sink", np.broadcast_to(i["attn_sinks"][order][None, :], (P, 8)))
    put("sinkd", np.broadcast_to(i["attn_sinks"].reshape(1, 8, 1), (4, 8, ST)).reshape(P, 1))
    put("wdw", i["conv_w_dw"].reshape(CW, KC, P).transpose(2, 1, 0).reshape(P, KC * CW))

    con = np.zeros((P, NCON), f32)
    con[:, 0:128] = np.eye(P)
    con[:, 128:256] = 1.0
    con[:, 256:384] = np.arange(P)[None, :]
    con[:, 384:399] = np.array(CAND_AT[1:])[None, :]
    con[:, 399:414] = np.diff(np.array(CAND_AT))[None, :]
    mcn = np.zeros((P, NMC), f32)
    r = np.arange(P)
    mcn[:, 0:128] = (r[:, None] // HD == r[None, :] // HD)
    rot = np.zeros((P, P), f32)
    for b in (0, HD):
        for a in range(8):
            rot[b + a + 8, b + a] = -1.0
            rot[b + a, b + a + 8] = 1.0
    mcn[:, 128:256] = rot
    qi, ki = np.arange(WIN)[:, None], np.arange(2 * WIN)[None, :]
    dist = qi + WIN - ki
    ok = (dist >= 0) & (dist < WIN)
    mcn[:, 256:512] = np.where(ok, 0.0, -1e30)
    mcn[:, 512:768] = np.where(ok & (ki >= WIN), 0.0, -1e30)
    dist = (WIN + r[:, None] % ST) - np.arange(WIN + ST)[None, :]
    mcn[:, 768:900] = np.where((dist >= 0) & (dist < WIN), 0.0, -1e30)
    mcn[:, 900:1028] = (r[:, None] <= r[None, :]) & (r[:, None] // 16 == r[None, :] // 16)
    rs = r[:NS]
    mcn[:NS, 1028:1060] = (rs[:, None] <= rs[None, :]) & (rs[:, None] // ST == rs[None, :] // ST)
    mcn[:, 1060:1068] = r[:, None] // 16 == np.arange(8)[None, :]
    mcn[:, 1068:1076] = r[:, None] // ST == np.arange(8)[None, :]
    inv = (f32(500000.0) ** (-np.arange(0, 16, 2, dtype=f32) / f32(16))).astype(f32)
    posn = np.concatenate([np.arange(NP), np.tile(1024 + np.arange(ST), SB)]).astype(f32)
    ang = (posn[:, None] * inv[None, :]).astype(f32)
    cos, sin = np.ones((P, NT), f32), np.zeros((P, NT), f32)
    for b in (0, 8, HD, HD + 8):
        cos[b:b + 8], sin[b:b + 8] = np.cos(ang).T, np.sin(ang).T
    mcn[:, 1076:1076 + NT], mcn[:, 1076 + NT:] = cos, sin
    reset = np.ones((P, NT), f32)
    for off, _ in CHUNKS:
        reset[:, off] = 0.0

    kc = i["cache_swa_k"].reshape(SB, WIN, P)
    vc = i["cache_swa_v"].reshape(SB, WIN, P)
    arrays = {
        "xT": xT, "stream": stream, "params": par, "consts": con, "mconsts": mcn, "reset": reset,
        "keysT": i["peer_keys"].reshape(2, 16, NKEY, P).transpose(0, 3, 1, 2),
        "kcacheT": kc.transpose(2, 0, 1), "vcache": vc.transpose(1, 0, 2), "kvcache_n": np.stack([kc, vc]),
        "state_h": i["state_hgrn"], "convT": i["state_conv"].transpose(2, 0, 1),
    }
    nc = _bacc.Bacc("TRN2", target_bir_lowering=False, num_devices=1)
    args, feed = [], {}
    for n, a in arrays.items():
        a = np.ascontiguousarray(a)
        feed[f"in_{n}"] = a
        args.append(nc.dram_tensor(f"in_{n}", a.shape, _mybir.dt.from_np(a.dtype), kind="ExternalInput").ap())
    for n, shape in _OUTS:
        args.append(nc.dram_tensor(f"out_{n}", shape, _mybir.dt.float32, kind="ExternalOutput").ap())
    build(nc, *args)
    o = _run(nc, [feed], core_ids=[0]).results[0]
    y = o["out_yT"].T
    return (y[:NP].reshape(1, NP, D), y[NP:].reshape(SB, ST, D),
            o["out_kwin_p"].reshape(1, WIN, 2, HD), o["out_vwin_p"].reshape(1, WIN, 2, HD),
            o["out_s_p"].reshape(1, 4, P, P), o["out_cb_p"].T.reshape(1, CW - 1, D),
            o["out_kwin_s"].reshape(SB, WIN, 2, HD), o["out_vwin_s"].reshape(SB, WIN, 2, HD),
            o["out_s_s"], o["out_cb_s"].transpose(1, 2, 0))
```
